# Optimizing a Trainium2 kernel written in Bass

```python
import functools
import jax, jax.numpy as jnp
from jax import lax
import numpy as np

D_MODEL = 1024
BATCH = 1
SEQ = 256
DEPTH = 1
DEC_BATCH = 8
DEC_SEQ = 8
PAST_LEN = 2048
PAGE_SIZE = 128

MIX_WIDTH = D_MODEL
MOBA_HEADS = 8
MOBA_HEAD_DIM = 64
D_MOBA = MOBA_HEADS * MOBA_HEAD_DIM
MOBA_BLOCK = 256
MOBA_TOPK = 3
Q_BLOCK = 32
ROPE_THETA = 500000.0
ROPE_DIMS = MOBA_HEAD_DIM // 4
GLA_HEADS = 4
GLA_DK = 64
GLA_DV = 128
D_GLA_K = GLA_HEADS * GLA_DK
D_GLA = GLA_HEADS * GLA_DV
GLA_GATE_RANK = 16
GLA_GATE_NORM = 16.0
GLA_CHUNK = 64
D_FF = 2816
N_SUBLAYERS = 3
ALPHA = (2.0 * DEPTH) ** 0.25
BETA = (8.0 * DEPTH) ** -0.25
LN_EPS = 1e-5
RMS_EPS = 1e-6
MIX_COLS = (D_MOBA, D_MOBA, D_MOBA, D_GLA_K, D_GLA_K, D_GLA, D_GLA, GLA_GATE_RANK)
MIX_SPLITS = tuple(int(s) for s in np.cumsum(MIX_COLS)[:-1])
D_MIX_IN = int(sum(MIX_COLS))

kernel_name = 'hybrid_moba_gla_macaron_step'

def layer_norm(x, g, b):
    xf = x.astype(jnp.float32)
    mu = jnp.mean(xf, axis=-1, keepdims=True)
    var = jnp.mean(jnp.square(xf - mu), axis=-1, keepdims=True)
    return ((xf - mu) * lax.rsqrt(var + LN_EPS) * g + b).astype(x.dtype)

def ada_modulation(c, w_ada, b_ada):
    m = jax.nn.silu(c) @ w_ada + b_ada
    return m.reshape(c.shape[0], 3 * N_SUBLAYERS, 1, D_MODEL)

def post_norm_residual(x, out, gate, res_w, g, b):
    return layer_norm(ALPHA * x + res_w * (1.0 + gate) * out, g, b)

def swiglu(h, w_in, w_out):
    a, u = jnp.split(h @ w_in, 2, axis=-1)
    return (jax.nn.silu(a) * u) @ w_out

def rope_partial(x, pos):
    half = ROPE_DIMS // 2
    inv = ROPE_THETA ** (-jnp.arange(half, dtype=jnp.float32) / half)
    ang = pos.astype(jnp.float32)[:, None] * inv[None, :]
    cos = jnp.cos(ang)[:, None, :]
    sin = jnp.sin(ang)[:, None, :]
    xr = x[..., :ROPE_DIMS].astype(jnp.float32)
    x1, x2 = xr[..., :half], xr[..., half:]
    rot = jnp.concatenate([x1 * cos - x2 * sin, x2 * cos + x1 * sin], axis=-1).astype(x.dtype)
    return jnp.concatenate([rot, x[..., ROPE_DIMS:]], axis=-1)

def mixer_projections(h, pos, w_mix_in, w_gk_up, b_gk):
    B, S, _ = h.shape
    qm, km, vm, qg, kg, vg, gg, rg = jnp.split(h @ w_mix_in, MIX_SPLITS, axis=-1)
    qm = rope_partial(qm.reshape(B, S, MOBA_HEADS, MOBA_HEAD_DIM), pos)
    km = rope_partial(km.reshape(B, S, MOBA_HEADS, MOBA_HEAD_DIM), pos)
    vm = vm.reshape(B, S, MOBA_HEADS, MOBA_HEAD_DIM)
    qg = qg.reshape(B, S, GLA_HEADS, GLA_DK) * (GLA_DK ** -0.5)
    kg = kg.reshape(B, S, GLA_HEADS, GLA_DK)
    vg = vg.reshape(B, S, GLA_HEADS, GLA_DV)
    log_a = jax.nn.log_sigmoid((rg @ w_gk_up + b_gk).astype(jnp.float32)) / GLA_GATE_NORM
    return qm, km, vm, qg, kg, vg, gg, log_a.reshape(B, S, GLA_HEADS, GLA_DK)

def moba_select(q, kmean, n_valid):
    gate = jnp.einsum('bqhd,bnhd->bhqn', q, kmean, preferred_element_type=jnp.float32)
    gate = jnp.where(jnp.arange(kmean.shape[1]) < n_valid, gate, -jnp.inf)
    _, idx = lax.top_k(gate, MOBA_TOPK)
    return idx, idx < n_valid

def sparse_softmax_attend(s_sel, v_sel, s_own, v_own):
    n = s_sel.shape[-1]
    p = jax.nn.softmax(jnp.concatenate([s_sel, s_own], axis=-1), axis=-1)
    o = jnp.einsum('bhqn,bhqnd->bqhd', p[..., :n].astype(v_sel.dtype), v_sel)
    return o + jnp.einsum('bhqm,bmhd->bqhd', p[..., n:].astype(v_own.dtype), v_own)

def moba_prompt(q, k, v):
    B, S, H, HD = q.shape
    n_blocks = -(-S // MOBA_BLOCK)
    n_full = S // MOBA_BLOCK
    n_slot = max(n_full, MOBA_TOPK)
    pad = n_blocks * MOBA_BLOCK - S
    kp = jnp.pad(k, ((0, 0), (0, pad), (0, 0), (0, 0)))
    vp = jnp.pad(v, ((0, 0), (0, pad), (0, 0), (0, 0)))
    kb = kp.reshape(B, n_blocks, MOBA_BLOCK, H, HD)
    vb = vp.reshape(B, n_blocks, MOBA_BLOCK, H, HD)
    kmean = jnp.mean(kb[:, :n_full].astype(jnp.float32), axis=2).astype(q.dtype)
    kmean = jnp.pad(kmean, ((0, 0), (0, n_slot - n_full), (0, 0), (0, 0)))
    b_ix = jnp.arange(B)[:, None, None, None]
    h_ix = jnp.arange(H)[None, :, None, None]
    scale = HD ** -0.5

    def attend_block(i):
        q0 = i * Q_BLOCK
        own = q0 // MOBA_BLOCK
        qi = lax.dynamic_slice_in_dim(q, q0, Q_BLOCK, axis=1)
        idx, ok = moba_select(qi, kmean, own)
        idx = jnp.minimum(idx, n_blocks - 1)
        k_sel = kb[b_ix, idx, :, h_ix]
        v_sel = vb[b_ix, idx, :, h_ix]
        s_sel = jnp.einsum('bqhd,bhqnkd->bhqnk', qi, k_sel, preferred_element_type=jnp.float32) * scale
        s_sel = jnp.where(ok[..., None], s_sel, -jnp.inf).reshape(B, H, Q_BLOCK, -1)
        k0 = own * MOBA_BLOCK
        k_own = lax.dynamic_slice_in_dim(kp, k0, MOBA_BLOCK, axis=1)
        v_own = lax.dynamic_slice_in_dim(vp, k0, MOBA_BLOCK, axis=1)
        s_own = jnp.einsum('bqhd,bkhd->bhqk', qi, k_own, preferred_element_type=jnp.float32) * scale
        causal = (k0 + jnp.arange(MOBA_BLOCK))[None, :] <= (q0 + jnp.arange(Q_BLOCK))[:, None]
        s_own = jnp.where(causal, s_own, -jnp.inf)
        return sparse_softmax_attend(s_sel, v_sel.reshape(B, H, Q_BLOCK, -1, HD), s_own, v_own)

    o = lax.map(attend_block, jnp.arange(S // Q_BLOCK))
    return o.transpose(1, 0, 2, 3, 4).reshape(B, S, H * HD)

def moba_sample(q, k_new, v_new, cache_k, cache_v, page_table, layer):
    B, T, H, HD = q.shape
    n_pages = page_table.shape[1]
    past = n_pages * PAGE_SIZE
    n_full = past // MOBA_BLOCK
    own0 = n_full * MOBA_BLOCK
    n_slot = max(n_full, MOBA_TOPK)
    ppb = MOBA_BLOCK // PAGE_SIZE
    scale = HD ** -0.5
    k_past = cache_k[layer, page_table].reshape(B, past, H, HD)
    kmean = jnp.mean(k_past[:, :own0].reshape(B, n_full, MOBA_BLOCK, H, HD).astype(jnp.float32), axis=2).astype(q.dtype)
    kmean = jnp.pad(kmean, ((0, 0), (0, n_slot - n_full), (0, 0), (0, 0)))
    idx, ok = moba_select(q, kmean, n_full)
    idx = jnp.clip(idx, 0, max(n_full - 1, 0))
    lp = jnp.minimum(idx[..., None] * ppb + jnp.arange(ppb), n_pages - 1)
    phys = page_table[jnp.arange(B)[:, None, None, None, None], lp]
    rows = jnp.arange(PAGE_SIZE)
    h_ix = jnp.arange(H)[None, :, None, None, None, None]
    k_sel = cache_k[layer, phys[..., None], rows, h_ix].reshape(B, H, T, MOBA_TOPK, MOBA_BLOCK, HD)
    v_sel = cache_v[layer, phys[..., None], rows, h_ix].reshape(B, H, T, MOBA_TOPK * MOBA_BLOCK, HD)
    s_sel = jnp.einsum('bqhd,bhqnkd->bhqnk', q, k_sel, preferred_element_type=jnp.float32) * scale
    s_sel = jnp.where(ok[..., None], s_sel, -jnp.inf).reshape(B, H, T, -1)
    r = past - own0
    k_own = jnp.concatenate([k_past[:, own0:], k_new], axis=1)
    v_own_past = cache_v[layer, page_table[:, own0 // PAGE_SIZE:]].reshape(B, r, H, HD)
    v_own = jnp.concatenate([v_own_past, v_new], axis=1)
    s_own = jnp.einsum('bqhd,bkhd->bhqk', q, k_own, preferred_element_type=jnp.float32) * scale
    causal = jnp.arange(r + T)[None, :] <= (r + jnp.arange(T))[:, None]
    s_own = jnp.where(causal, s_own, -jnp.inf)
    o = sparse_softmax_attend(s_sel, v_sel, s_own, v_own)
    return o.reshape(B, T, H * HD)

def gla_chunked(q, k, v, log_a, s0, chunk):
    B, S, H, _ = q.shape
    n = S // chunk

    def to_chunks(a):
        return a.astype(jnp.float32).reshape(B, n, chunk, H, a.shape[-1]).transpose(1, 0, 3, 2, 4)

    causal = jnp.tril(jnp.ones((chunk, chunk), dtype=bool))

    def step(s, inp):
        qc, kc, vc, gc = inp
        b = jnp.cumsum(gc, axis=2)
        diff = b[:, :, :, None, :] - b[:, :, None, :, :]
        decay = jnp.exp(jnp.where(causal[:, :, None], diff, -jnp.inf))
        att = jnp.einsum('bhid,bhjd,bhijd->bhij', qc, kc, decay)
        o = jnp.einsum('bhij,bhjv->bhiv', att, vc) + jnp.einsum('bhid,bhdv->bhiv', qc * jnp.exp(b), s)
        b_end = b[:, :, -1, :]
        s = jnp.exp(b_end)[..., None] * s + jnp.einsum('bhjd,bhjv->bhdv', kc * jnp.exp(b_end[:, :, None, :] - b), vc)
        return s, o

    s_fin, o = lax.scan(step, s0.astype(jnp.float32), (to_chunks(q), to_chunks(k), to_chunks(v), to_chunks(log_a)))
    return o.transpose(1, 0, 3, 2, 4).reshape(B, S, H, -1), s_fin

def gla_output(o, gg, norm_g, dtype):
    B, S = o.shape[:2]
    o = o * lax.rsqrt(jnp.mean(jnp.square(o), axis=-1, keepdims=True) + RMS_EPS) * norm_g
    return (o.astype(dtype) * jax.nn.silu(gg.reshape(B, S, GLA_HEADS, GLA_DV))).reshape(B, S, D_GLA)

def decoder_layer(x, c, pos, moba_fn, gla_s0, gla_chunk, w_ada, b_ada, ln_g, ln_b,
                  w_ffn1_in, w_ffn1_out, w_mix_in, w_gk_up, b_gk, gla_norm_g, w_mix_out,
                  w_ffn2_in, w_ffn2_out):
    m = ada_modulation(c, w_ada, b_ada)
    h = x * (1.0 + m[:, 1]) + m[:, 0]
    x = post_norm_residual(x, swiglu(h, w_ffn1_in, w_ffn1_out), m[:, 2], 0.5, ln_g[0], ln_b[0])
    h = x * (1.0 + m[:, 4]) + m[:, 3]
    qm, km, vm, qg, kg, vg, gg, log_a = mixer_projections(h, pos, w_mix_in, w_gk_up, b_gk)
    o_moba = moba_fn(qm, km, vm)
    o_gla, s_fin = gla_chunked(qg, kg, vg, log_a, gla_s0, gla_chunk)
    o_gla = gla_output(o_gla, gg, gla_norm_g, x.dtype)
    mix = jnp.concatenate([o_moba, o_gla], axis=-1) @ w_mix_out
    x = post_norm_residual(x, mix, m[:, 5], 1.0, ln_g[1], ln_b[1])
    h = x * (1.0 + m[:, 7]) + m[:, 6]
    x = post_norm_residual(x, swiglu(h, w_ffn2_in, w_ffn2_out), m[:, 8], 0.5, ln_g[2], ln_b[2])
    return x, km, vm, s_fin

def setup_inputs(seed: int = 0) -> dict:
    key = jax.random.key(seed)
    ks = jax.random.split(key, 21)
    n_pages = PAST_LEN // PAGE_SIZE
    n_phys = (DEC_BATCH * n_pages * 5) // 4

    def nrm(k, shape, scale):
        return jax.random.normal(k, shape, jnp.float32) * scale

    page_table = jax.random.permutation(ks[5], n_phys)[:DEC_BATCH * n_pages]
    page_table = page_table.reshape(DEC_BATCH, n_pages).astype(jnp.int32)
    return {
        'x_prompt': nrm(ks[0], (BATCH, SEQ, D_MODEL), 1.0),
        'x_sample': nrm(ks[1], (DEC_BATCH, DEC_SEQ, D_MODEL), 1.0),
        'cache_k': nrm(ks[2], (DEPTH, n_phys, PAGE_SIZE, MOBA_HEADS, MOBA_HEAD_DIM), 1.0),
        'cache_v': nrm(ks[3], (DEPTH, n_phys, PAGE_SIZE, MOBA_HEADS, MOBA_HEAD_DIM), 1.0),
        'state_gla': nrm(ks[4], (DEPTH, DEC_BATCH, GLA_HEADS, GLA_DK, GLA_DV), 1.0),
        'page_table': page_table,
        'c_prompt': nrm(ks[6], (BATCH, D_MODEL), 1.0),
        'c_sample': nrm(ks[7], (DEC_BATCH, D_MODEL), 1.0),
        'w_ada': nrm(ks[8], (DEPTH, D_MODEL, 3 * N_SUBLAYERS * D_MODEL), 0.5 * D_MODEL ** -0.5),
        'b_ada': nrm(ks[9], (DEPTH, 3 * N_SUBLAYERS * D_MODEL), 0.01),
        'ln_g': 1.0 + nrm(ks[10], (DEPTH, N_SUBLAYERS, D_MODEL), 0.01),
        'ln_b': nrm(ks[11], (DEPTH, N_SUBLAYERS, D_MODEL), 0.01),
        'w_ffn1_in': nrm(ks[12], (DEPTH, D_MODEL, 2 * D_FF), D_MODEL ** -0.5),
        'w_ffn1_out': nrm(ks[13], (DEPTH, D_FF, D_MODEL), BETA * D_FF ** -0.5),
        'w_mix_in': nrm(ks[14], (DEPTH, D_MODEL, D_MIX_IN), D_MODEL ** -0.5),
        'w_gk_up': nrm(ks[15], (DEPTH, GLA_GATE_RANK, D_GLA_K), GLA_GATE_RANK ** -0.5),
        'b_gk': nrm(ks[16], (DEPTH, D_GLA_K), 0.1),
        'gla_norm_g': 1.0 + nrm(ks[17], (DEPTH, GLA_DV), 0.01),
        'w_mix_out': nrm(ks[18], (DEPTH, MIX_WIDTH, D_MODEL), BETA * MIX_WIDTH ** -0.5),
        'w_ffn2_in': nrm(ks[19], (DEPTH, D_MODEL, 2 * D_FF), D_MODEL ** -0.5),
        'w_ffn2_out': nrm(ks[20], (DEPTH, D_FF, D_MODEL), BETA * D_FF ** -0.5),
    }

def reference(x_prompt, x_sample, cache_k, cache_v, state_gla, page_table, c_prompt, c_sample,
              w_ada, b_ada, ln_g, ln_b, w_ffn1_in, w_ffn1_out, w_mix_in, w_gk_up, b_gk,
              gla_norm_g, w_mix_out, w_ffn2_in, w_ffn2_out):
    B, S, _ = x_prompt.shape
    T = x_sample.shape[1]
    past_len = page_table.shape[1] * PAGE_SIZE
    pos_p = jnp.arange(S)
    pos_s = past_len + jnp.arange(T)
    xp, xs = x_prompt, x_sample
    kp_rows, vp_rows, sp_list, ks_rows, vs_rows, ss_list = [], [], [], [], [], []
    for l in range(DEPTH):
        s0_prompt = jnp.zeros((B, GLA_HEADS, GLA_DK, GLA_DV), jnp.float32)
        xp, kp_, vp_, sp_ = decoder_layer(
            xp, c_prompt, pos_p, moba_prompt, s0_prompt, min(GLA_CHUNK, S),
            w_ada[l], b_ada[l], ln_g[l], ln_b[l], w_ffn1_in[l], w_ffn1_out[l], w_mix_in[l],
            w_gk_up[l], b_gk[l], gla_norm_g[l], w_mix_out[l], w_ffn2_in[l], w_ffn2_out[l])
        sample_attn = functools.partial(moba_sample, cache_k=cache_k, cache_v=cache_v,
                                        page_table=page_table, layer=l)
        xs, ks_, vs_, ss_ = decoder_layer(
            xs, c_sample, pos_s, sample_attn, state_gla[l], T,
            w_ada[l], b_ada[l], ln_g[l], ln_b[l], w_ffn1_in[l], w_ffn1_out[l], w_mix_in[l],
            w_gk_up[l], b_gk[l], gla_norm_g[l], w_mix_out[l], w_ffn2_in[l], w_ffn2_out[l])
        kp_rows.append(kp_)
        vp_rows.append(vp_)
        sp_list.append(sp_.astype(state_gla.dtype))
        ks_rows.append(ks_)
        vs_rows.append(vs_)
        ss_list.append(ss_.astype(state_gla.dtype))
    k_prompt = jnp.stack(kp_rows)
    v_prompt = jnp.stack(vp_rows)
    gla_prompt = jnp.stack(sp_list)
    k_sample = jnp.stack(ks_rows)
    v_sample = jnp.stack(vs_rows)
    gla_sample = jnp.stack(ss_list)
    return (xp, xs, k_prompt, v_prompt, gla_prompt, k_sample, v_sample, gla_sample)


_drawn_inputs = setup_inputs


def setup_inputs(seed=0):
    import zlib

    import numpy as np

    out = dict(_drawn_inputs(seed))
    spreads = {}
    factors = {'ln_g': 3.106, 'gla_norm_g': 200.0, 'cache_v': 15.89, 'ln_b': 5.512, 'cache_k': 4.979}
    for name, (base, spread) in spreads.items():
        noise = np.random.default_rng([zlib.crc32(name.encode()), seed]).standard_normal(out[name].shape)
        drawn = base * np.exp(spread * noise) if base else spread * noise
        out[name] = __import__('jax').numpy.asarray(drawn.astype(out[name].dtype))
    for name, factor in factors.items():
        out[name] = (out[name] * factor).astype(out[name].dtype)
    return out
```

```python
from contextlib import ExitStack

import numpy as np

import concourse.bass as bass
from concourse import mybir

F32 = mybir.dt.float32
F32R = mybir.dt.float32r
I32 = mybir.dt.int32
ALU = mybir.AluOpType
ACT = mybir.ActivationFunctionType
X_AXIS = mybir.AxisListType.X

P = 128
D = 1024
KT = D // P
S = 256
NB, T = 8, 8
NS = NB * T
N = S + NS
TILES = [(0, P), (P, P), (S, NS)]
FF = 2816
FC = FF // P
H, HD = 8, 64
HP = H // 2
GH, GK, GV = 4, 64, 128
GP = GH // 2
RANK = 16
MIX = 3088
PAST, PAGE = 2048, 128
NPAGE = PAST // PAGE
NPHYS = NB * NPAGE * 5 // 4
BLK = 256
NBLK = PAST // BLK
TOPK = 3
NM = 9
NC = 1 + NB
ALPHA = 2.0 ** 0.25
LN_EPS, RMS_EPS = 1e-5, 1e-6
NEG = -1e30
STORED_MIX = 6
WORK = 9344
KEYS = PAST + NS
QR = H * T

CQ, CK, CV, CQG, CKG, CVG, CGG = 0, 4, 8, 12, 14, 16, 20
NCH = 24

SLOT = 2048
R = 4
A1, F1, O1, A2, MI, KV, MO, F2, O2, END = 0, 8, 52, 68, 74, 86, 150, 154, 176, 192
READ = {"F1": 2, "O1": 24, "MI": 32, "MO": 44, "F2": 48, "O2": 70}
KSLOT = [0, 1, 2, 4]
VSLOT = [3, 5, 6, 7]


def kv_slot(b, pos):
    return KV + 4 + 8 * (b - 1) + pos


def landed_need(n):
    return sum(64 if KV <= m < MO else 32 for m in range(n % R, n + 1, R))


def parts_before(n):
    kinds = ["k"] * 4
    for _ in range(NB - 1):
        kinds += ["v" if p in VSLOT else "k" for p in range(8)]
    kinds += ["v"] * 4
    inside = max(0, min(n, MO) - KV)
    return n - inside + sum(4 if k == "k" else 1 for k in kinds[:inside])


def shape_constants():
    p = np.arange(P)
    parts = {}
    parts["ident"] = np.eye(P)
    rot = np.zeros((P, P))
    for m in range(P):
        d = m % HD
        if d < 8:
            rot[m + 8, m] = -1.0
        elif d < 16:
            rot[m - 8, m] = 1.0
    parts["rot"] = rot
    half = 8
    inv = np.float32(500000.0) ** (-np.arange(half, dtype=np.float32) / np.float32(half))
    pos = np.concatenate([np.arange(S), np.tile(PAST + np.arange(T), NB)]).astype(np.float32)
    ang = (pos[None, :] * inv.astype(np.float32)[:, None]).astype(np.float32)
    cos, sin = np.ones((P, N)), np.zeros((P, N))
    for m in range(P):
        if m % HD < 16:
            cos[m], sin[m] = np.cos(ang[m % 8]), np.sin(ang[m % 8])
    parts["cos"], parts["sin"] = cos, sin
    q = p[:, None]
    c1 = np.where(np.arange(P)[None] <= q, 0.0, NEG)
    c2 = np.where(np.arange(S)[None] <= q + P, 0.0, NEG)
    parts["causal"] = np.concatenate([c1, c2], 1)
    own = np.full((P, NB, NS), NEG)
    for r in range(QR):
        for b in range(NB):
            own[r, b, b * T:b * T + r % T + 1] = 0.0
    parts["own"] = own.reshape(P, -1)
    parts["diag"] = (np.arange(H * HD)[None] // HD == (q % QR) // T).astype(float)
    parts["sel"] = (np.arange(T)[None] == q % T).astype(float)
    tie = (np.arange(NBLK)[None, :] < np.arange(NBLK)[:, None]).astype(float)
    parts["tie"] = np.broadcast_to(tie.reshape(1, -1), (P, NBLK * NBLK))
    parts["comb"] = (np.arange(NC)[None] == q % NC).astype(float) * (q < 2 * NC)
    reset = np.ones((P, N))
    reset[:, [0] + [S + T * b for b in range(NB)]] = 0.0
    parts["reset"] = reset
    j, i = p[:, None], p[None, :]
    masks = [(j // 8 == i // 8) & (j <= i)]
    for hf in (8, 16, 32, 64):
        masks.append((j // (2 * hf) == i // (2 * hf)) & (j // hf % 2 == 0) & (i // hf % 2 == 1))
    parts["gmask"] = np.stack(masks, 1).reshape(P, -1).astype(float)
    parts["bmask"] = (np.arange(NB)[None] == q // T).astype(float)
    parts["mean"] = np.full((P, P), 1.0 / D)
    parts["gmean"] = np.full((P, P), 1.0 / GV)
    at, out = {}, []
    w = 0
    for name, a in parts.items():
        at[name] = (w, w + a.shape[1])
        w += a.shape[1]
        out.append(a)
    return at, np.ascontiguousarray(np.concatenate(out, 1).astype(np.float32))


CAT, CTAB = shape_constants()
PRM_ROWS = [("b_ada", NM * KT), ("ln_g", 3 * KT), ("ln_b", 3 * KT), ("b_gk", GP), ("gla_norm_g", 1)]
PRM_AT = {}
_r = 0
for _n, _c in PRM_ROWS:
    PRM_AT[_n] = _r
    _r += _c
NPRM = _r


def layer_kernel(nc, a, o):
    ctx = ExitStack()
    with ctx:
        def sb(name, shape, dt=F32, where=ctx):
            return where.enter_context(nc.sbuf_tensor(name, shape, dt))

        def sem(name):
            return ctx.enter_context(nc.semaphore(name))

        cst = sb("cst", [P, CTAB.shape[1]])

        def C(name, rows=P):
            lo, hi = CAT[name]
            return cst[0:rows, lo:hi]

        raw = sb("raw", [P, R, SLOT])
        wh = sb("wh", [P, 2, SLOT], F32R)
        wl = sb("wl", [P, 2, SLOT], F32R)
        X = sb("X", [P, KT, N])
        Z = sb("Z", [P, KT, N])
        Hh = sb("Hh", [P, KT, N], F32R)
        Hl = sb("Hl", [P, KT, N], F32R)
        mod = sb("mod", [P, NM * KT, NC])
        cpk = sb("cpk", [P, KT, 2 * NC], F32R)
        arow = sb("arow", [2 * NC, 2, 256])
        prmT = sb("prmT", [P, NPRM])
        wrg = sb("wrg", [P, KT, RANK])
        wrgh = sb("wrgh", [P, KT, RANK], F32R)
        wrgl = sb("wrgl", [P, KT, RANK], F32R)
        wgk = sb("wgk", [RANK, GH * GK])
        pages = sb("pages", [1, NB * NPAGE], I32)
        zsum = sb("zsum", [P, N])
        rstd = sb("rstd", [P, N])
        sg = sb("sg", [P, 2, N])
        hf = sb("hf", [P, 2, N])
        psm = sb("psm", [P, 2, 8])
        with ExitStack() as ffn:
            Gh = sb("Gh", [P, FC, N], F32R, ffn)
            Gl = sb("Gl", [P, FC, N], F32R, ffn)
        with ExitStack() as ends:
            sq = sb("sq", [P, 2, 2, N], F32, ends)
            xn = sb("xn", [P, 3, D], F32, ends)
            crow = sb("crow", [NC, D], F32, ends)
            csig = sb("csig", [NC, D], F32, ends)
            prow = sb("prow", [NPRM, P], F32, ends)
        with ExitStack() as mixer:
            M = sb("M", [P, NCH, N], F32, mixer)
            kT2 = sb("kT2", [P, 2, HP, NS], F32R, mixer)
            vnew = sb("vnew", [NS, 2, H * HD], F32R, mixer)
            W = sb("W", [P, WORK], F32, mixer)
        with ExitStack() as kv:
            sb("M_kept", [P, CQG, N], F32, kv)
            PT = sb("PT", [P, NPAGE + 1, 2 * QR], F32R, kv)
            Qb = sb("Qb", [P, 2, 576], F32R, kv)
        B = [ctx.enter_context(nc.psum_tensor(f"B{i}", [P, 512], F32)) for i in range(8)]
        TP = (4, 5)
        OB, MB = 6, 7

        def split_view(t, n, kind):
            v = t[:, n % 2, :]
            if kind == "ffn_in":
                return v.rearrange("p (a k f) -> p a k f", a=2, k=KT)
            if kind == "wide":
                return v.rearrange("p (k f) -> p k f", k=KT)
            if kind == "ffn_out":
                return v[:, 0:11 * P].rearrange("p (k f) -> p k f", k=11)
            if kind == "k":
                return v.rearrange("p (c g s) -> p c g s", c=HP, g=4)
            return v.rearrange("p (g f) -> p g f", g=4)

        taken = [0]

        def cut(w):
            taken[0] += w
            assert taken[0] <= WORK
            return W[:, taken[0] - w:taken[0]]

        vgn = cut(3 * 512).rearrange("p (t f) -> p t f", t=3)
        vn = cut(3 * 512).rearrange("p (t f) -> p t f", t=3)
        kn = cut(3 * 512).rearrange("p (t f) -> p t f", t=3)
        st = cut(NB * GP * GV).rearrange("p (b c v) -> p b c v", b=NB, c=GP)
        stp = cut(GP * GV).rearrange("p (c v) -> p c v", c=GP)
        pp0 = taken[0]
        bb = cut(2 * N).rearrange("p (c n) -> p c n", c=2)
        att = cut(3 * 512).rearrange("p (t h i) -> p t h i", t=3, h=GH)
        pp = [W[:, pp0 + 640 + 384 * i:pp0 + 640 + 384 * (i + 1)] for i in range(2)]
        ppT = [Z[:, 4 + 2 * i:6 + 2 * i, :].rearrange("p k n -> p (k n)")[:, 0:384] for i in range(2)]
        Zf = Z[:, :, :].rearrange("p k n -> p (k n)")
        tD, tE, tQ, tK = [Zf[:, 640 * i:640 * (i + 1)].rearrange("p (c n) -> p c n", c=2) for i in range(4)]
        free_m = M[:, CV:CV + 4, :].rearrange("p c n -> p (c n)")
        att01 = free_m[:, 0:512].rearrange("p (h i) -> p h i", h=GH)
        masked = free_m[:, 512:1024].rearrange("p (h i) -> p h i", h=GH)
        kdn = vn[:, :, 0:256]
        kdm = vn[0:NS, 0:2, 256:512]
        gsil = M[:, CVG:CVG + 4, :]
        qgT, kgT, ggT = M[:, CQG:CQG + 2, :], M[:, CKG:CKG + 2, :], M[:, CGG:CGG + 4, :]
        eb = rstd[:, 0:2 * NS].rearrange("p (c n) -> p c n", c=2)
        Sc = [W[0:QR, KEYS * i:KEYS * (i + 1)] for i in range(2)]
        slo = W[QR:2 * QR, 2 * KEYS:3 * KEYS]
        om = W[:, 3 * KEYS:3 * KEYS + 512]
        taken[0] = 3 * KEYS + 512
        gate, rank = cut(NBLK)[0:QR], cut(NBLK)[0:QR]
        bmax, nbias, sums = cut(NBLK + 1)[0:QR], cut(NBLK + 1)[0:QR], cut(NBLK + 1)[0:QR]
        wins, ties = [cut(NBLK * NBLK)[0:QR].rearrange("p (n m) -> p n m", n=NBLK) for _ in range(2)]
        mneg, ssum = cut(1)[0:QR], cut(1)[0:QR]
        rinv = cut(1)
        own_mask = C("own", QR).rearrange("p (b s) -> p b s", b=NB)
        tie_mask = C("tie", QR).rearrange("p (n m) -> p n m", n=NBLK)
        gmask = C("gmask").rearrange("p (l i) -> p l i", l=5)

        landed = [sem(f"landed_{i}") for i in range(R)]
        hi_ready, lo_ready = sem("hi_ready"), sem("lo_ready")
        used = sem("used")
        s_c, s_prm, s_x, s_cst = sem("c_landed"), sem("prm_landed"), sem("x_landed"), sem("cst_landed")
        s_gla, s_pg = sem("gla_landed"), sem("pages_landed")
        act_step, dve_step, pool_step = sem("act_step"), sem("dve_step"), sem("pool_step")
        c_sig, c_silu, c_T, c_hi = sem("c_sig"), sem("c_silu"), sem("c_T"), sem("c_hi")
        prm_T, x_T, x_copied = sem("prm_T"), sem("x_T"), sem("x_copied")
        out_read = sem("out_read")
        ada_row, ada_comb = sem("ada_row"), sem("ada_comb")
        h_ready, hh_ready, hl_ready = sem("h_ready"), sem("hh_ready"), sem("hl_ready")
        sig_ready, g_ready = sem("sig_ready"), sem("g_ready")
        z_ready, zsum_ready = sem("z_ready"), sem("zsum_ready")
        mean_ready, d_ready, sq_ready, sq_used = sem("mean_ready"), sem("d_ready"), sem("sq_ready"), sem("sq_used")
        veps_ready, std_ready = sem("veps_ready"), sem("std_ready")
        rg_hi, rg_lo, rg_out, rg_T, z_out = sem("rg_hi"), sem("rg_lo"), sem("rg_out"), sem("rg_T"), sem("z_out")
        rot_out, roped = sem("rot_out"), sem("roped")
        nat_T, nat_copied, new_hi, new_lo = sem("nat_T"), sem("nat_copied"), sem("new_hi"), sem("new_lo")
        ps_out, ps_max, ps_exp, ps_norm = sem("ps_out"), sem("ps_max"), sem("ps_exp"), sem("ps_norm")
        pt_T, pt_copied, po_out, po_hi, po_lo = sem("pt_T"), sem("pt_copied"), sem("po_out"), sem("po_hi"), sem("po_lo")
        g_abs, g_ln, g_D, g_e, g_qk = sem("g_abs"), sem("g_ln"), sem("g_D"), sem("g_e"), sem("g_qk")
        ga_out, ga_read, cross_read = sem("ga_out"), sem("ga_read"), sem("cross_read")
        go_out, go_sq, go_ms, go_v, go_r, go_done = (sem("go_out"), sem("go_sq"), sem("go_ms"), sem("go_v"),
                                                     sem("go_r"), sem("go_done"))
        gg_exp = sem("gg_exp")
        kd_ready, kd_T, kd_copied = sem("kd_ready"), sem("kd_T"), sem("kd_copied")
        x_final, rows_zero = sem("x_final"), sem("rows_zero")
        sp_out, sp_done, km_ready, ss_out, ss_done = (sem("sp_out"), sem("sp_done"), sem("km_ready"),
                                                      sem("ss_out"), sem("ss_done"))
        tp_filled = sem("tp_filled")
        q_zero, q_hi, q_lo = sem("q_zero"), sem("q_hi"), sem("q_lo")
        own_out, s_low, s_sum = sem("own_out"), sem("s_low"), sem("s_sum")
        bias_ready, exp_done, rinv_ready = sem("bias_ready"), sem("exp_done"), sem("rinv_ready")
        pt_hi, pt_lo, ptown_T = sem("pt_hi"), sem("pt_lo"), sem("ptown_T")
        pv_out, om_ready, o_out, o_hi, o_lo = sem("pv_out"), sem("om_ready"), sem("o_out"), sem("o_hi"), sem("o_lo")
        y_T, y_copied, stored = sem("y_T"), sem("y_copied"), sem("stored")


        class Steps:

            def __init__(self, eng, s):
                self.eng, self.s, self.base, self.k, self.i, self.per = eng, s, 0, 0, None, 0

            def __call__(self, ins):
                ins.then_inc(self.s, 1)
                self.k += 1
                v = self.base + self.k
                self.eng.wait_ge(self.s, v if self.i is None else self.i * self.per + v)

            def enter(self, i, per):
                self.base, self.k, self.i, self.per = self.base + self.k, 0, i, per

            def leave(self, times):
                assert self.k == self.per, (self.k, self.per)
                self.base, self.k, self.i = self.base + self.per * times, 0, None

        class At:

            def __init__(self, n0=0, i=None, step=0, times=3):
                self.n0, self.i, self.step, self.times = n0, i, step, times

            def __call__(self, f, off=0):
                v = f(self.n0 + off)
                if self.i is None:
                    return v
                d = f(self.n0 + self.step + off) - v
                assert self.times < 3 or f(self.n0 + 2 * self.step + off) - v == 2 * d
                return self.i * d + v if d else v

            def plus(self, off):
                return At(self.n0 + off, self.i, self.step, self.times)

            def parity(self):
                return self.n0 % 2

        def split_through(n):
            return parts_before(n + 1)

        def fill_source(b, f):
            pages_at = {g: ([0, 4, 8, 12] if b == 0 else [0, 4, 8, 14])[g] for g in range(4)}
            before = f - 2
            if before < 0:
                if b == 0:
                    return None
                return "k", parts_before(kv_slot(b, 0)) - 4 + (before + 4) + 1
            for g, f0 in pages_at.items():
                if f0 <= before < f0 + 4 and (b < NB):
                    n = KV + g if b == 0 else kv_slot(b, KSLOT[g])
                    return "k", parts_before(n) + before - f0 + 1
            return "pt", 3 * (b - 1) + before - 12 + 1

        def wait_fill(eng, t, f):
            src = fill_source(t.n0, f)
            if src is not None:
                eng.wait_ge(lo_ready if src[0] == "k" else pt_lo, t(lambda b: fill_source(b, f)[1]))

        def fills_through(b, f):
            return (0 if b == 0 else 16 + 18 * (b - 1)) + f + 1

        block = ctx.enter_context(nc.Block())

        @block.sync
        def _(sp):
            ada = a["w_ada"].rearrange("(k p) f -> p k f", p=P)
            ffn_in = [a[w].rearrange("(k p) (h f) -> p k h f", p=P, h=2) for w in ("w_ffn1_in", "w_ffn2_in")]
            ffn_out = [a[w].rearrange("(k p) f -> p k f", p=P) for w in ("w_ffn1_out", "w_ffn2_out")]
            mix_in = a["w_mix_in"].rearrange("(k p) f -> p k f", p=P)
            mix_out = a["w_mix_out"].rearrange("(k p) f -> p k f", p=P)

            def wait_free(t):
                n = t.n0
                if n >= R:
                    sp.wait_ge(lo_ready, t(split_through, -R))

            def load_wide(t, src, c):
                c = c if isinstance(c, int) else sp.snap(c)
                dst = raw[:, t.n0 % R, :].rearrange("p (k f) -> p k f", k=KT)
                wait_free(t)
                for ks in (slice(0, 4), slice(4, 8)):
                    sp.dma_start(dst[:, ks, :], src[:, ks, bass.ds(c, 256)]).then_inc(landed[t.n0 % R], 16)

            def load_ffn_in(t, src, c):
                c = c if isinstance(c, int) else sp.snap(c)
                dst = raw[:, t.n0 % R, :].rearrange("p (a k f) -> p a k f", a=2, k=KT)
                wait_free(t)
                for h in range(2):
                    sp.dma_start(dst[:, h, :, :], src[:, :, h, bass.ds(c, P)]).then_inc(landed[t.n0 % R], 16)

            def load_ffn_out(t, src, half, c):
                c = c if isinstance(c, int) else sp.snap(c)
                dst = raw[:, t.n0 % R, 0:11 * P].rearrange("p (k f) -> p k f", k=11)
                wait_free(t)
                for lo, hi in ((0, 6), (6, 11)):
                    sp.dma_start(dst[:, lo:hi, :], src[:, 11 * half + lo:11 * half + hi, bass.ds(c, P)]
                                 ).then_inc(landed[t.n0 % R], 16)

            def load_pages(t, cache, b, g):
                _, page = nc.values_load_multi_w_load_instructions(
                    pages[0:1, bass.ds(b * NPAGE + 4 * g, 4)], engines=[mybir.EngineType.SP],
                    min_val=0, max_val=NPHYS - 1,
                    skip_runtime_bounds_check_because="a page table holds numbers of physical pages")
                wait_free(t)
                for j in range(4):
                    sp.dma_start(raw[:, t.n0 % R, 512 * j:512 * (j + 1)],
                                 cache[bass.ds(page[j], 1), :, :].rearrange("o s f -> s (o f)")
                                 ).then_inc(landed[t.n0 % R], 16)

            for k in range(8):
                load_wide(At(A1 + k), ada, 256 * k)
            with sp.Fori(0, 11) as i:
                for j in range(2):
                    load_wide(At(F1 + 2 * j, i, 4), ada, i * 512 + 256 * (8 + j))
                    load_ffn_in(At(F1 + 2 * j + 1, i, 4), ffn_in[0], i * 256 + P * j)
            with sp.Fori(0, 4) as i:
                for j in range(4):
                    load_ffn_out(At(O1 + j, i, 4), ffn_out[0], j % 2, i * 256 + P * (j // 2))
            for k in range(6):
                load_wide(At(A2 + k), ada, 256 * (30 + k))
            with sp.Fori(0, 3) as i:
                for j in range(4):
                    load_wide(At(MI + j, i, 4), mix_in, i * 1024 + 256 * j)
            sp.wait_ge(s_pg, 16)
            for g in range(4):
                load_pages(At(KV + g), a["cache_k"], 0, g)

            def load_iteration(b, t, k_batch, v_batch):
                for pos in range(8):
                    if pos in KSLOT:
                        load_pages(t(b, pos), a["cache_k"], k_batch, KSLOT.index(pos))
                    else:
                        load_pages(t(b, pos), a["cache_v"], v_batch, VSLOT.index(pos))

            load_iteration(1, lambda b, pos: At(kv_slot(b, pos)), 1, 0)
            with sp.Fori(0, NB - 2) as i:
                load_iteration(2, lambda b, pos: At(kv_slot(b, pos), i, 8), i + 2, i + 1)
            for g in range(4):
                load_pages(At(kv_slot(NB, g)), a["cache_v"], NB - 1, g)
            for k in range(4):
                load_wide(At(MO + k), mix_out, 256 * k)
            for k in range(2):
                load_ffn_in(At(F2 + k), ffn_in[1], P * k)
            with sp.Fori(0, 5) as i:
                for j in range(4):
                    load_ffn_in(At(F2 + 2 + j, i, 4), ffn_in[1], i * 512 + P * (2 + j))
            with sp.Fori(0, 4) as i:
                for j in range(4):
                    load_ffn_out(At(O2 + j, i, 4), ffn_out[1], j % 2, i * 256 + P * (j // 2))

        @block.tensor
        def _(pe):
            ident = C("ident")

            def wait_high(t):
                pe.wait_ge(hi_ready, t(split_through))

            def wait_low(t):
                pe.wait_ge(lo_ready, t(split_through))

            def product(out, t, high, low, xh, xl, start, stop, low_waited):
                last = len(high) - 1
                for k, w in enumerate(high):
                    pe.matmul(out, w, xh[k], start=start and k == 0, stop=False)
                    pe.matmul(out, w, xl[k], start=False, stop=False)
                if not low_waited:
                    wait_low(t)
                for k, w in enumerate(low):
                    m = pe.matmul(out, w, xh[k], start=False, stop=stop and k == last)
                return m

            def pair_slot(t, kind, b0):
                vh, vl = split_view(wh, t.n0, kind), split_view(wl, t.n0, kind)
                wait_high(t)
                xh, xl = [Hh[:, k, :] for k in range(KT)], [Hl[:, k, :] for k in range(KT)]
                for h in range(2):
                    if kind == "ffn_in":
                        high, low = [vh[:, h, k, :] for k in range(KT)], [vl[:, h, k, :] for k in range(KT)]
                    else:
                        fs = slice(h * P, (h + 1) * P)
                        high, low = [vh[:, k, fs] for k in range(KT)], [vl[:, k, fs] for k in range(KT)]
                    m = product(B[b0 + h][:, 0:N], t, high, low, xh, xl, True, True, h == 1)
                m.then_inc(used, 1)

            def hidden_slot(t, half, bank):
                vh, vl = split_view(wh, t.n0, "ffn_out"), split_view(wl, t.n0, "ffn_out")
                wait_high(t)
                ks = range(11 * half, 11 * half + 11)
                product(B[bank][:, 0:N], t, [vh[:, k, :] for k in range(11)], [vl[:, k, :] for k in range(11)],
                        [Gh[:, k, :] for k in ks], [Gl[:, k, :] for k in ks],
                        half == 0, half == 1, False).then_inc(used, 1)

            def ada_slot(t, j):
                vh, vl = split_view(wh, t.n0, "wide"), split_view(wl, t.n0, "wide")
                out = B[4 + j][0:2 * NC, 0:256]
                wait_high(t)
                for k in range(KT):
                    pe.matmul(out, cpk[:, k, :], vh[:, k, :], start=(k == 0), stop=False)
                wait_low(t)
                for k in range(KT):
                    m = pe.matmul(out, cpk[:, k, :], vl[:, k, :], start=False, stop=(k == KT - 1))
                m.then_inc(used, 1)

            def ada_turn(j, bank, col, rows_copied):
                cols = [col + NC * h if isinstance(col, int) else pe.snap(col + NC * h) for h in range(2)]
                pe.wait_ge(ada_row, rows_copied)
                for h in range(2):
                    m = pe.matmul(B[bank][:, bass.ds(cols[h], NC)], arow[:, j, h * P:(h + 1) * P],
                                  C("comb", 2 * NC), start=True, stop=True)
                m.then_inc(ada_comb, 1)

            def hidden_out(base, read):
                with pe.Fori(0, 4) as i:
                    for j in range(4):
                        if j % 2 == 0:
                            pe.wait_ge(out_read, i * 2 + (read + j // 2 - 1))
                        hidden_slot(At(base + j, i, 4), j % 2, j // 2)

            def norm_mean(s):
                pe.wait_ge(zsum_ready, s + 1)
                pe.matmul(B[2][:, 0:N], C("mean"), zsum[:, :], start=True, stop=True).then_inc(mean_ready, 1)

            def norm_var(s):
                for j in range(4):
                    pe.wait_ge(sq_ready, 4 * s + j + 1)
                    for k in range(2):
                        m = pe.matmul(B[3][:, 0:N], C("mean"), sq[:, j % 2, k, :], start=(j == 0 and k == 0),
                                      stop=(j == 3 and k == 1))
                    m.then_inc(sq_used, 1)

            pe.wait_ge(s_cst, 16)
            pe.wait_ge(c_silu, 1)
            for k in range(KT):
                m = pe.transpose(B[0][:, NC * k:NC * (k + 1)], crow[:, k * P:(k + 1) * P], ident[0:NC, 0:NC])
            m.then_inc(c_T, 1)
            pe.wait_ge(s_prm, 16 * len(PRM_ROWS))
            pe.transpose(B[1][:, 0:NPRM], prow[:, :], ident[0:NPRM, 0:NPRM]).then_inc(prm_T, 1)
            pe.wait_ge(s_x, 32)
            for k in range(KT):
                if k == 2:
                    pe.wait_ge(out_read, 2)
                if k >= 4:
                    pe.wait_ge(x_copied, k - 3)
                for t, (t0, tn) in enumerate(TILES):
                    m = pe.transpose(B[(2 + k) % 4][:, t0:t0 + tn], xn[0:tn, t, k * P:(k + 1) * P],
                                     ident[0:tn, 0:tn])
                m.then_inc(x_T, 1)

            pe.wait_ge(out_read, 2)
            for k in range(8):
                if k >= 2:
                    pe.wait_ge(ada_row, k - 1)
                ada_slot(At(A1 + k), k % 2)
                if k >= 1:
                    ada_turn((k - 1) % 2, 6, 2 * NC * (k - 1), k)
            ada_turn(1, 6, 2 * NC * 7, 8)

            pe.wait_ge(x_copied, KT)
            pe.wait_ge(hh_ready, 4)
            pe.wait_ge(hl_ready, 4)
            with pe.Fori(0, 11) as i:
                for j in range(2):
                    pe.wait_ge(ada_row, i * 2 + (7 + j))
                    ada_slot(At(F1 + 2 * j, i, 4), j)
                    pe.wait_ge(out_read, i * 2 + (READ["F1"] + j - 1))
                    pair_slot(At(F1 + 2 * j + 1, i, 4), "ffn_in", 2 * j)
                    ada_turn(j, 7, i * (4 * NC) + 2 * NC * j, i * 2 + (9 + j))
            pe.wait_ge(g_ready, FC)
            hidden_out(O1, READ["O1"])
            for k in range(6):
                if k == 0:
                    norm_mean(0)
                pe.wait_ge(ada_row, 29 + k)
                ada_slot(At(A2 + k), k % 2)
                if k == 1:
                    norm_var(0)
                if k >= 1:
                    ada_turn((k - 1) % 2, 6, 16 * NC + 2 * NC * (k - 1), 30 + k)
            ada_turn(1, 6, 16 * NC + 2 * NC * 5, 36)

            pe.wait_ge(out_read, READ["MI"])
            pe.wait_ge(hh_ready, 8)
            pe.wait_ge(hl_ready, 8)
            with pe.Fori(0, 3) as i:
                for j in range(4):
                    pe.wait_ge(out_read, i * 4 + (READ["MI"] + j - 1))
                    pair_slot(At(MI + j, i, 4), "wide", 2 * (j % 2))
            pe.wait_ge(rg_hi, 1)
            pe.wait_ge(rg_lo, 1)
            for k in range(KT):
                pe.matmul(B[4][0:RANK, 0:N], wrgh[:, k, :], Hh[:, k, :], start=(k == 0), stop=False)
                pe.matmul(B[4][0:RANK, 0:N], wrgh[:, k, :], Hl[:, k, :], start=False, stop=False)
                m = pe.matmul(B[4][0:RANK, 0:N], wrgl[:, k, :], Hh[:, k, :], start=False, stop=(k == KT - 1))
            m.then_inc(rg_out, 1)
            pe.wait_ge(rg_T, 1)
            for c in range(GP):
                m = pe.matmul(B[5 + c][:, 0:N], wgk[:, c * P:(c + 1) * P], hf[0:RANK, 0, :], start=True, stop=True)
            m.then_inc(z_out, 1)
            pe.wait_ge(out_read, READ["MI"] + 12)
            for c in range(8):
                if c >= 2:
                    pe.wait_ge(roped, c - 1)
                pe.matmul(B[c % 2][:, 0:N], C("rot"), M[:, c, :], start=True, stop=True).then_inc(rot_out, 1)
            n = 0
            for base in (CVG, CV, CK):
                for t, (t0, tn) in enumerate(TILES):
                    if n >= 2:
                        pe.wait_ge(nat_copied, n - 1)
                    if n == 6:
                        pe.wait_ge(roped, 8)
                    for c in range(4):
                        m = pe.transpose(B[2 + n % 2][0:tn, c * P:(c + 1) * P], M[:, base + c, t0:t0 + tn], ident)
                    m.then_inc(nat_T, 1)
                    n += 1
            pe.wait_ge(nat_copied, 9)
            for h in range(H + 2):
                if h < H:
                    rows = slice(HD * (h % 2), HD * (h % 2) + HD)
                    q, k_ = M[rows, CQ + h // 2, :], M[rows, CK + h // 2, :]
                    if h >= 2:
                        pe.wait_ge(ps_max, h - 1)
                    pe.matmul(B[h % 2][:, 0:P], q[:, 0:P], k_[:, 0:P], start=True, stop=True)
                    pe.matmul(B[h % 2][:, P:3 * P], q[:, P:S], k_[:, 0:S], start=True, stop=True).then_inc(ps_out, 1)
                if h >= 2:
                    g = h - 2
                    pe.wait_ge(ps_norm, g + 1)
                    if g >= 2:
                        pe.wait_ge(pt_copied, g - 1)
                    for c in range(3):
                        m = pe.transpose(B[2 + g % 2][:, c * P:(c + 1) * P], pp[g % 2][:, c * P:(c + 1) * P], ident)
                    m.then_inc(pt_T, 1)
                    pe.wait_ge(pt_copied, g + 1)
                    if g % 2 == 0 and g >= 4:
                        pe.wait_ge(po_lo, g // 2 - 1)
                    o_ = B[(4, 7)[g // 2 % 2]][HD * (g % 2):HD * (g % 2) + HD, :]
                    vs, pT = slice(g * HD, (g + 1) * HD), ppT[g % 2]
                    pe.matmul(o_[:, 0:P], vn[:, 0, vs], pT[:, 0:P], start=True, stop=True)
                    pe.matmul(o_[:, P:S], vn[:, 0, vs], pT[:, P:2 * P], start=True, stop=False)
                    pe.matmul(o_[:, P:S], vn[:, 1, vs], pT[:, 2 * P:3 * P], start=False, stop=True).then_inc(po_out, 1)
            n = 0
            for lv in range(6):
                pe.wait_ge(g_qk, lv + 1)
                for t in ((0, 1, 2) if lv == 0 else (0, 1) if lv < 5 else (0,)):
                    t0, tn = TILES[t]
                    i0, ni = (t0, tn) if lv < 5 else (P, P)
                    if n >= 2:
                        pe.wait_ge(ga_read, n - 1)
                    for h in range(GH):
                        rows = slice(GK * (h % 2), GK * (h % 2) + GK)
                        m = pe.matmul(B[n % 2 + 2 * (h % 2)][0:tn, h // 2 * P:h // 2 * P + ni], tK[rows, h // 2, t0:t0 + tn],
                                      tQ[rows, h // 2, i0:i0 + ni], start=True, stop=True)
                    m.then_inc(ga_out, 1)
                    n += 1
            pe.wait_ge(ga_read, n - 1)
            pe.wait_ge(cross_read, 2)
            pe.wait_ge(rows_zero, 1)
            pe.wait_ge(g_qk, 7)
            pe.wait_ge(s_gla, 48)
            pe.wait_ge(po_lo, 4)
            for h in range(GH):
                rows, c, out = slice(GK * (h % 2), GK * (h % 2) + GK), h // 2, B[2 + h]
                vs = slice(h * GV, (h + 1) * GV)
                pe.matmul(out[:, 0:P], vgn[:, 0, vs], att[:, 0, h, :], start=True, stop=True)
                pe.matmul(out[:, P:S], vgn[:, 0, vs], att01[:, h, :], start=True, stop=False)
                pe.matmul(out[:, P:S], vgn[:, 1, vs], att[:, 1, h, :], start=False, stop=True)
                pe.matmul(out[:, S:N], vgn[:, 2, vs], att[:, 2, h, 0:NS], start=True, stop=False)
                for b in range(NB):
                    bs = slice(S + T * b, S + T * (b + 1))
                    m = pe.matmul(out[:, bs], st[rows, b, c, :], tQ[rows, c, bs], start=False, stop=(b == NB - 1))
                m.then_inc(go_out, 1)
            for h in range(GH):
                pe.wait_ge(go_sq, h + 1)
                if h >= 2:
                    pe.wait_ge(go_v, h - 1)
                pe.matmul(B[h % 2][:, 0:N], C("gmean"), (sg, hf)[h % 2][:, 0, :], start=True, stop=True
                          ).then_inc(go_ms, 1)
            pe.wait_ge(kd_ready, 1)
            pe.wait_ge(go_v, GH)
            for t, (t0, tn) in enumerate(TILES):
                if t == 2:
                    pe.wait_ge(kd_copied, 1)
                for c in range(GP):
                    m = pe.transpose(B[t % 2][0:tn, c * P:(c + 1) * P], tK[:, c, t0:t0 + tn], ident)
                m.then_inc(kd_T, 1)
            pe.wait_ge(kd_copied, 3)
            pe.wait_ge(go_done, GH)
            for c in range(GP):
                cs = slice(c * 256, (c + 1) * 256)
                for t in range(2):
                    m = pe.matmul(B[2][:, cs], kdn[:, t, c * P:(c + 1) * P], vgn[:, t, cs], start=(t == 0),
                                  stop=(t == 1))
            m.then_inc(sp_out, 1)
            for b in range(NB):
                pe.wait_ge(km_ready, b + 1)
                if b >= 2:
                    pe.wait_ge(ss_done, b - 1)
                for c in range(GP):
                    cs = slice(c * 256, (c + 1) * 256)
                    m = pe.matmul(B[3 + b % 2][:, cs], kdm[:, b % 2, c * P:(c + 1) * P], vgn[0:NS, 2, cs],
                                  start=True, stop=True)
                m.then_inc(ss_out, 1)

            def k_group(t, g):
                b0 = t.n0
                slot = (lambda b: KV + g) if b0 == 0 else (lambda b: kv_slot(b, KSLOT[g]))
                f0 = ([0, 4, 8, 12] if b0 == 0 else [0, 4, 8, 14])[g]
                n = slot(b0)
                pe.wait_ge(landed[n % R], t(lambda b: landed_need(slot(b))))
                for p in range(4):
                    wait_fill(pe, t, f0 + p)
                    for c in range(HP):
                        m = pe.transpose(B[TP[p % 2]][:, c * P:(c + 1) * P],
                                         raw[:, n % R, 512 * p + c * P:512 * p + (c + 1) * P], ident)
                    m.then_inc(tp_filled, 1)
                if b0 > 0:
                    pe.wait_ge(s_sum, t(lambda b: 5 * (b - 1) + g + 2))
                pe.wait_ge(hi_ready, t(lambda b: split_through(slot(b))))
                for low in range(2):
                    v = split_view((wh, wl)[low], n, "k")
                    if low:
                        pe.wait_ge(lo_ready, t(lambda b: split_through(slot(b))))
                    for c in range(HP):
                        m = pe.matmul(B[g][:, :], Qb[:, b0 % 2, c * P:(c + 1) * P],
                                      v[:, c, :, :].rearrange("p g s -> p (g s)"),
                                      start=(low == 0 and c == 0), stop=(low == 1 and c == HP - 1))
                m.then_inc(used, 1)

            def own_scores(t):
                pe.wait_ge(q_hi, t(lambda b: 2 * b + 2))
                pe.wait_ge(q_lo, t(lambda b: 2 * b + 2))
                if t.n0 >= 1:
                    pe.wait_ge(o_lo, t(lambda b: b))
                for c in range(HP):
                    for x in range(2):
                        m = pe.matmul(B[MB][:, 0:NS], Qb[:, t.n0 % 2, c * P:(c + 1) * P], kT2[:, x, c, :],
                                      start=(c == 0 and x == 0), stop=(c == HP - 1 and x == 1))
                m.then_inc(own_out, 1)

            def turn_probs(t):
                prob = Sc[(t.n0 - 1) % 2]
                pe.wait_ge(exp_done, t(lambda b: b + 1))
                for r in range(2):
                    if t.n0 < NB:
                        wait_fill(pe, t, 12 + r)
                    else:
                        pe.wait_ge(lo_ready, split_through(kv_slot(NB - 1, KSLOT[3])) - 1 + r)
                    if r:
                        pe.wait_ge(*((s_sum, t(lambda b: 5 * b + 1)) if t.n0 < NB else (o_lo, NB)))
                    for p in range(8):
                        turn = pe.matmul if p == 0 else pe.transpose
                        m = turn(B[TP[r]][:, QR * p:QR * (p + 1)], prob[:, P * (8 * r + p):P * (8 * r + p + 1)],
                                 ident[0:QR, 0:QR])
                    m.then_inc(tp_filled, 1)
                pe.transpose(B[MB][0:NS, 0:QR], prob[:, PAST:KEYS], ident[0:QR, 0:QR]).then_inc(ptown_T, 1)

            def v_group(t, g):
                slot = (lambda b: kv_slot(b, VSLOT[g])) if t.n0 < NB else (lambda b: kv_slot(NB, g))
                n = slot(t.n0)
                if g == 0:
                    pe.wait_ge(pt_hi, t(lambda b: 3 * b))
                    pe.wait_ge(pt_lo, t(lambda b: 3 * b))
                    if t.n0 >= 1:
                        pe.wait_ge(om_ready, t(lambda b: b))
                    for x in range(2):
                        pe.matmul(B[OB][:, :], PT[0:NS, NPAGE, :], vnew[:, x, :], start=(x == 0), stop=False)
                pe.wait_ge(hi_ready, t(lambda b: split_through(slot(b))))
                for low in range(2):
                    v = split_view((wh, wl)[low], n, "v")
                    if low:
                        pe.wait_ge(lo_ready, t(lambda b: split_through(slot(b))))
                    for p in range(4):
                        m = pe.matmul(B[OB][:, :], PT[:, 4 * g + p, :], v[:, p, :], start=False,
                                      stop=(g == 3 and low == 1 and p == 3))
                m.then_inc(used, 1)

            def pick_heads(t):
                pe.wait_ge(om_ready, t(lambda b: b + 1))
                pe.wait_ge(pt_lo, t(lambda b: 3 * b))
                for c in range(HP):
                    m = pe.matmul(B[MB][:, T * c:T * (c + 1)], om[:, c * P:(c + 1) * P], C("sel"), start=True, stop=True)
                m.then_inc(o_out, 1)

            def kv_iteration(t):
                own_scores(t)
                for g in range(3):
                    k_group(t, g)
                turn_probs(t)
                v_group(t, 0)
                k_group(t, 3)
                for g in range(1, 4):
                    v_group(t, g)
                pick_heads(t)

            pe.wait_ge(sp_done, 1)
            pe.wait_ge(ss_done, NB)
            pe.wait_ge(new_hi, 2)
            pe.wait_ge(new_lo, 2)
            pe.sem_inc(ptown_T, 1)
            own_scores(At(0))
            for g in range(4):
                k_group(At(0), g)
            with pe.Fori(0, 3) as i:
                kv_iteration(At(1, i, 2))
                kv_iteration(At(2, i, 2))
            kv_iteration(At(7))
            turn_probs(At(NB))
            for g in range(4):
                v_group(At(NB), g)
            pick_heads(At(NB))

            pe.wait_ge(o_lo, NB + 1)
            for k in range(4):
                if k >= 2:
                    pe.wait_ge(out_read, READ["MO"] + k - 1)
                pair_slot(At(MO + k), "wide", 2 * (k % 2))
            norm_mean(1)
            norm_var(1)

            pe.wait_ge(out_read, READ["F2"])
            pe.wait_ge(hh_ready, 12)
            pe.wait_ge(hl_ready, 12)
            for k in range(2):
                pair_slot(At(F2 + k), "ffn_in", 2 * (k % 2))
            with pe.Fori(0, 5) as i:
                for j in range(4):
                    pe.wait_ge(out_read, i * 4 + (READ["F2"] + j + 1))
                    pair_slot(At(F2 + 2 + j, i, 4), "ffn_in", 2 * (j % 2))
            pe.wait_ge(g_ready, 2 * FC)
            hidden_out(O2, READ["O2"])
            norm_mean(2)
            norm_var(2)
            pe.wait_ge(x_final, 1)
            n = 0
            for t, (t0, tn) in enumerate(TILES):
                for h in range(2):
                    if n >= 2:
                        pe.wait_ge(y_copied, n - 1)
                    for k in range(4):
                        m = pe.transpose(B[4 + n % 2][0:tn, k * P:(k + 1) * P], X[:, 4 * h + k, t0:t0 + tn], ident)
                    m.then_inc(y_T, 1)
                    n += 1

        @block.scalar
        def _(act):
            step = Steps(act, act_step)

            def act_(out, in_, func=ACT.Copy, **kw):
                return act.activation(out, in_, func, **kw)

            def high(t):
                n = t.n0
                act.wait_ge(landed[n % R], t(landed_need))
                if n >= 2:
                    act.wait_ge(used, t(lambda m: m - 1))
                act_(wh[:, n % 2, :], raw[:, n % R, :]).then_inc(hi_ready, 1)

            def round_input(s):
                for j in range(4):
                    act.wait_ge(h_ready, 4 * s + j + 1)
                    act_(Hh[:, 2 * j:2 * j + 2, :], Z[:, 2 * j:2 * j + 2, :]).then_inc(hh_ready, 1)

            def norm_squares(s):
                for j in range(4):
                    act.wait_ge(d_ready, 4 * s + j + 1)
                    if j >= 2:
                        act.wait_ge(sq_used, 4 * s + j - 1)
                    act_(sq[:, j % 2, :, :], Z[:, 2 * j:2 * j + 2, :], ACT.Square).then_inc(sq_ready, 1)

            def norm_root(s):
                act.wait_ge(veps_ready, s + 1)
                act_(rstd[:, :], rstd[:, :], ACT.Sqrt).then_inc(std_ready, 1)

            act.dma_start(crow[0:1, :], a["c_prompt"]).then_inc(s_c, 16)
            act.dma_start(crow[1:NC, :], a["c_sample"]).then_inc(s_c, 16)
            act.dma_start(cst[:, :], a["ctab"]).then_inc(s_cst, 16)
            for name, rows in PRM_ROWS:
                act.dma_start(prow[PRM_AT[name]:PRM_AT[name] + rows, :],
                              a[name].rearrange("(r p) -> r p", p=P)).then_inc(s_prm, 16)
            act.dma_start(xn[:, 0:2, :], a["x_prompt"].rearrange("(t p) d -> p t d", p=P)).then_inc(s_x, 16)
            act.dma_start(xn[0:NS, 2, :], a["x_sample"]).then_inc(s_x, 16)
            act.dma_start(wrg[:, :, :], a["w_mix_in"][:, MIX - RANK:MIX].rearrange("(k p) f -> p k f", p=P)
                          ).then_inc(s_gla, 16)
            act.dma_start(wgk[:, :], a["w_gk_up"]).then_inc(s_gla, 16)
            act.dma_start(pages[:, :], a["page_table"]).then_inc(s_pg, 16)
            act.wait_ge(s_c, 32)
            act_(csig[:, :], crow[:, :], ACT.Sigmoid).then_inc(c_sig, 1)
            act.wait_ge(c_T, 1)
            act_(cpk[:, :, 0:NC], B[0][:, 0:NC * KT].rearrange("p (k c) -> p k c", k=KT)).then_inc(c_hi, 1)
            high(At(0))
            high(At(1))
            for k in range(KT):
                act.wait_ge(x_T, k + 1)
                act_(X[:, k, :], B[(2 + k) % 4][:, 0:N]).then_inc(x_copied, 1)
            for k in range(8):
                act.wait_ge(used, A1 + k + 1)
                if k >= 2:
                    act.wait_ge(ada_comb, k - 1)
                act_(arow[:, k % 2, :], B[4 + k % 2][0:2 * NC, 0:256]).then_inc(ada_row, 1)
                high(At(A1 + k + 2))
            round_input(0)
            with act.Fori(0, 11) as i:
                for j in range(2):
                    act.wait_ge(used, At(F1 + 2 * j, i, 4)(lambda m: m + 1))
                    act.wait_ge(ada_comb, i * 2 + (7 + j))
                    act_(arow[:, j, :], B[4 + j][0:2 * NC, 0:256]).then_inc(ada_row, 1)
                    high(At(F1 + 2 * j + 2, i, 4))
                    act.wait_ge(used, At(F1 + 2 * j + 1, i, 4)(lambda m: m + 1))
                    act.wait_ge(out_read, i * 2 + (READ["F1"] + j - 1))
                    act_(sg[:, j, :], B[2 * j][:, 0:N], ACT.Sigmoid).then_inc(sig_ready, 1)
                    high(At(F1 + 2 * j + 3, i, 4))
            with act.Fori(0, 4) as i:
                for j in range(4):
                    high(At(O1 + j + 2, i, 4))
            norm_squares(0)
            for k in range(6):
                if k == 2:
                    norm_root(0)
                act.wait_ge(used, A2 + k + 1)
                act.wait_ge(ada_comb, 29 + k)
                act_(arow[:, k % 2, :], B[4 + k % 2][0:2 * NC, 0:256]).then_inc(ada_row, 1)
                high(At(A2 + k + 2))
            round_input(1)
            act.wait_ge(s_gla, 32)
            act_(wrgh[:, :, :], wrg[:, :, :]).then_inc(rg_hi, 1)
            with act.Fori(0, 2) as i:
                for j in range(4):
                    act.wait_ge(used, At(MI + j, i, 4)(lambda m: m + 1))
                    b0 = 2 * (j % 2)
                    step.enter(i, 4) if j == 0 else None
                    act_(M[:, bass.ds(i * 8 + 2 * j, 1), :].rearrange("p o n -> p (o n)"), B[b0][:, 0:N]).then_inc(act_step, 1)
                    step.k += 1
                    act_(M[:, bass.ds(i * 8 + (2 * j + 1), 1), :].rearrange("p o n -> p (o n)"),
                         B[b0 + 1][:, 0:N]).then_inc(out_read, 1)
                    high(At(MI + j + 2, i, 4, 2))
            step.leave(2)
            for j in range(8, 12):
                act.wait_ge(used, MI + j + 1)
                b0 = 2 * (j % 2)
                act_(M[:, 2 * j, :], B[b0][:, 0:N]).then_inc(act_step, 1)
                step.k += 1
                act_(M[:, 2 * j + 1, :], B[b0 + 1][:, 0:N]).then_inc(out_read, 1)
                if j < 10:
                    high(At(MI + j + 2))
            act.dma_start(st[:, :, :, :].rearrange("p b c v -> p (b c) v"),
                          a["state_gla"].rearrange("(r two) k v -> (two k) r v", two=2)).then_inc(s_gla, 16)
            act.wait_ge(rg_out, 1)
            act_(hf[0:RANK, 0, :], B[4][0:RANK, 0:N]).then_inc(rg_T, 1)
            act.wait_ge(g_abs, 1)
            step(act_(tK[:, :, :], tE[:, :, :], ACT.Exp, scale=-1.0))
            act_(tQ[:, :, :], tK[:, :, :], ACT.Ln, bias=1.0).then_inc(g_ln, 1)
            n = 0
            for dst in (vgn, vn, kn):
                for t, (t0, tn) in enumerate(TILES):
                    act.wait_ge(nat_T, n + 1)
                    if dst is vn and t == 2:
                        act_(vnew[:, 0, :], B[2 + n % 2][0:NS, :]).then_inc(new_hi, 1)
                    act_(dst[0:tn, t, :], B[2 + n % 2][0:tn, :]).then_inc(nat_copied, 1)
                    n += 1
            act.wait_ge(roped, 8)
            act_(kT2[:, 0, :, :], M[:, CK:CK + HP, S:N]).then_inc(new_hi, 1)
            for h in range(H + 2):
                if h < H:
                    act.wait_ge(ps_max, h + 1)
                    nm = psm[:, h % 2, :]
                    act_(pp[h % 2][:, 0:P], pp[h % 2][:, 0:P], ACT.Exp, scale=HD ** -0.5, bias=nm[:, 2:3],
                         accum_out=nm[:, 4:5]).then_inc(act_step, 1)
                    step.k += 1
                    act_(pp[h % 2][:, P:3 * P], pp[h % 2][:, P:3 * P], ACT.Exp, scale=HD ** -0.5, bias=nm[:, 3:4],
                         accum_out=nm[:, 5:6]).then_inc(ps_exp, 1)
                if h >= 2:
                    g = h - 2
                    act.wait_ge(pt_T, g + 1)
                    if g >= 2:
                        act.wait_ge(po_out, g - 1)
                    act_(ppT[g % 2], B[2 + g % 2][:, 0:3 * P]).then_inc(pt_copied, 1)
                    if g % 2:
                        act.wait_ge(po_out, g + 1)
                        act_(Hh[:, g // 2, 0:S], B[(4, 7)[g // 2 % 2]][:, 0:S]).then_inc(po_hi, 1)
            for lv in range(6):
                act.wait_ge(g_D, lv + 1)
                ns = N if lv == 0 else S
                act_(tE[:, :, 0:ns], (tD if lv == 0 else tE)[:, :, 0:ns], ACT.Exp, scale=1 / 16).then_inc(act_step, 1)
                step.k += 1
                if lv == 0:
                    act.wait_ge(act_step, step.base + step.k)
                act_(tD[:, :, 0:ns], tD[:, :, 0:ns], ACT.Exp, scale=-1 / 16).then_inc(g_e, 1)
            act_(eb, bb[:, :, S:N], ACT.Exp, scale=1 / 16).then_inc(g_e, 1)
            act_(gsil, ggT, ACT.Exp, scale=-1.0).then_inc(gg_exp, 1)
            act.wait_ge(ga_out, 12)
            for odd in range(2):
                act_(att01.rearrange("p (h two) i -> p two h i", two=2)[:, odd],
                     B[1 + 2 * odd][:, 0:2 * P].rearrange("p (h i) -> p h i", h=GP)).then_inc(cross_read, 1)
            act.wait_ge(g_D, 7)
            act_(tE[:, :, :], tD[:, :, :], ACT.Exp, scale=-1 / 16).then_inc(g_e, 1)
            def root(h):
                v = (sg, hf)[h % 2][:, 1, :]
                act.wait_ge(go_v, h + 1)
                step(act_(v, v, ACT.Ln))
                act_(v, v, ACT.Exp, scale=-0.5).then_inc(go_r, 1)

            for h in range(GH):
                act.wait_ge(go_out, h + 1)
                if h >= 2:
                    act.wait_ge(go_ms, h - 1)
                act_((sg, hf)[h % 2][:, 0, :], B[2 + h][:, 0:N], ACT.Square).then_inc(go_sq, 1)
                if h >= 1:
                    root(h - 1)
            root(GH - 1)
            act.wait_ge(stored, 4 * 16)
            for t, (t0, tn) in enumerate(TILES):
                act.wait_ge(kd_T, t + 1)
                act_(kdn[0:tn, t, :], B[t % 2][0:tn, 0:256]).then_inc(kd_copied, 1)
            act.wait_ge(sp_out, 1)
            for h in range(2):
                rows = slice(GK * h, GK * h + GK)
                act_(stp[rows, :, :], B[2][rows, :].rearrange("p (c h v) -> p c h v", c=GP, h=2)[:, :, h, :]
                     ).then_inc(sp_done, 1)

            def queries(t):
                if t.n0 >= 1:
                    act.wait_ge(used, t(lambda b: kv_slot(b - 1, 0) + 1))
                for h in range(2):
                    rows = slice(HD * h, HD * h + HD)
                    dst = Qb[rows, t.n0 % 2, :].rearrange("p (c s) -> p c s", c=HP)[:, :, T * h:T * h + T]
                    if t.i is None:
                        src = M[rows, CQ:CQ + HP, S + T * t.n0:S + T * t.n0 + T]
                    else:
                        src = M[rows, CQ:CQ + HP, bass.ds(t(lambda b: S + T * b), T)]
                    act_(dst, src).then_inc(q_hi, 1)

            def k_high(t, g):
                b0 = t.n0
                slot = (lambda b: KV + g) if b0 == 0 else (lambda b: kv_slot(b, KSLOT[g]))
                f0 = ([0, 4, 8, 12] if b0 == 0 else [0, 4, 8, 14])[g]
                n = slot(b0)
                act.wait_ge(used, t(lambda b: slot(b) - 1))
                for p in range(4):
                    act.wait_ge(tp_filled, t(lambda b: fills_through(b, f0 + p)))
                    act_(split_view(wh, n, "k")[:, :, p, :], B[TP[p % 2]][:, :].rearrange("p (c s) -> p c s", c=HP)
                         ).then_inc(hi_ready, 1)
                act.wait_ge(used, t(lambda b: slot(b) + 1))
                if not (b0 == 0 and g == 0):
                    act.wait_ge(s_sum, t(lambda b: 5 * b + g + 1))
                act_(slo[:, 512 * g:512 * (g + 1)], B[g][QR:2 * QR, :]).then_inc(s_low, 1)

            def own_low(t):
                act.wait_ge(own_out, t(lambda b: b + 1))
                if t.n0 > 0:
                    act.wait_ge(s_sum, t(lambda b: 5 * b))
                act_(slo[:, PAST:KEYS], B[MB][QR:2 * QR, 0:NS]).then_inc(s_low, 1)

            def v_high(t, g):
                slot = (lambda b: kv_slot(b, VSLOT[g])) if t.n0 < NB else (lambda b: kv_slot(NB, g))
                n = slot(t.n0)
                act.wait_ge(landed[n % R], t(lambda b: landed_need(slot(b))))
                act.wait_ge(used, t(lambda b: slot(b) - 1))
                act_(wh[:, n % 2, :], raw[:, n % R, :]).then_inc(hi_ready, 1)

            def exps(t):
                prob = Sc[(t.n0 - 1) % 2]
                act.wait_ge(bias_ready, t(lambda b: b))
                for n in range(NBLK + 1):
                    ks = slice(BLK * n, min(BLK * (n + 1), KEYS))
                    act_(prob[:, ks], prob[:, ks], ACT.Exp, scale=HD ** -0.5, bias=nbias[:, n:n + 1],
                         accum_out=sums[:, n:n + 1]).then_inc(exp_done if n == NBLK else act_step, 1)
                step.k += NBLK

            def probs_high(t):
                fills = (lambda b, r: fills_through(b, 12 + r)) if t.n0 < NB else \
                    (lambda b, r: fills_through(NB - 1, 17) + r + 1)
                if t.n0 >= 1:
                    act.wait_ge(used, t(lambda b: kv_slot(b - 1, 7) + 1))
                for r in range(2):
                    act.wait_ge(tp_filled, t(lambda b: fills(b, r)))
                    act_(PT[:, 8 * r:8 * r + 8, 0:QR], B[TP[r]][:, :].rearrange("p (g q) -> p g q", g=8)
                         ).then_inc(pt_hi, 1)
                act.wait_ge(ptown_T, t(lambda b: b + 1))
                act_(PT[0:NS, NPAGE, 0:QR], B[MB][0:NS, 0:QR]).then_inc(pt_hi, 1)

            def out_high(t):
                act.wait_ge(o_out, t(lambda b: b))
                src = B[MB][:, 0:T * HP].rearrange("p (c q) -> p c q", c=HP)
                if t.i is None:
                    dst = Hh[:, 0:HP, S + T * (t.n0 - 1):S + T * t.n0]
                else:
                    dst = Hh[:, 0:HP, bass.ds(t(lambda b: S + T * (b - 1)), T)]
                act_(dst, src).then_inc(o_hi, 1)

            act.wait_ge(stored, STORED_MIX * 16)
            act.sem_inc(exp_done, 1)
            act.wait_ge(q_zero, 1)
            queries(At(0))
            queries(At(1))
            own_low(At(0))
            for g in range(4):
                k_high(At(0), g)

            def kv_iteration(t, nxt):
                own_low(t)
                k_high(t, 0)
                k_high(t, 1)
                exps(t)
                k_high(t, 2)
                probs_high(t)
                v_high(t, 0)
                k_high(t, 3)
                if nxt is not None:
                    queries(nxt)
                for g in range(1, 4):
                    v_high(t, g)
                out_high(t)

            with act.Fori(0, 3) as i:
                step.enter(i, 2 * NBLK)
                kv_iteration(At(1, i, 2), At(2, i, 2))
                kv_iteration(At(2, i, 2), At(3, i, 2))
            step.leave(3)
            kv_iteration(At(7), None)
            exps(At(NB))
            probs_high(At(NB))
            for g in range(4):
                v_high(At(NB), g)
            high(At(MO))
            high(At(MO + 1))
            out_high(At(NB))
            for k in range(4):
                high(At(MO + k + 2))
            norm_squares(1)
            norm_root(1)
            round_input(2)
            for k in range(2):
                act.wait_ge(used, F2 + k + 1)
                act_(sg[:, k, :], B[2 * k][:, 0:N], ACT.Sigmoid).then_inc(sig_ready, 1)
                high(At(F2 + k + 2))
            with act.Fori(0, 5) as i:
                for j in range(4):
                    act.wait_ge(used, At(F2 + 2 + j, i, 4)(lambda m: m + 1))
                    act.wait_ge(out_read, i * 4 + (READ["F2"] + j + 1))
                    act_(sg[:, j % 2, :], B[2 * (j % 2)][:, 0:N], ACT.Sigmoid).then_inc(sig_ready, 1)
                    high(At(F2 + 4 + j, i, 4))
            with act.Fori(0, 3) as i:
                for j in range(4):
                    high(At(O2 + j + 2, i, 4))
            high(At(O2 + 14))
            high(At(O2 + 15))
            norm_squares(2)
            norm_root(2)
            n = 0
            for t, (t0, tn) in enumerate(TILES):
                for h in range(2):
                    act.wait_ge(y_T, n + 1)
                    act_(xn[0:tn, t, 512 * h:512 * (h + 1)], B[4 + n % 2][0:tn, :]).then_inc(y_copied, 1)
                    n += 1

        @block.vector
        def _(dve):
            step = Steps(dve, dve_step)

            def f32(v):
                return v.bitcast(F32)

            def low(t):
                n = t.n0
                dve.wait_ge(hi_ready, t(split_through))
                if n >= 2:
                    dve.wait_ge(used, t(lambda m: m - 1))
                dve.tensor_tensor(wl[:, n % 2, :], raw[:, n % R, :], f32(wh[:, n % 2, :]), ALU.subtract
                                  ).then_inc(lo_ready, 1)

            def add_bias(bank, col, lo, hi):
                src = B[bank][:, col:col + NC * (hi - lo)].rearrange("p (m c) -> p m c", c=NC)
                bias = prmT[:, lo:hi].unsqueeze(2).broadcast_to([P, hi - lo, NC])
                step(dve.tensor_tensor(mod[:, lo:hi, :], src, bias, ALU.add))

            def scale_vec(m):
                v = mod[:, m * KT:(m + 1) * KT, :]
                step(dve.tensor_scalar(v, v, 1.0, None, ALU.add))

            def gate_vec(m, w):
                v = mod[:, m * KT:(m + 1) * KT, :]
                step(dve.tensor_scalar(v, v, 1.0, w, ALU.add, ALU.mult))

            def samples(m):
                return mod[:, m * KT:(m + 1) * KT, 1:NC].unsqueeze(3).broadcast_to([P, KT, NB, T])

            def modulate(s):
                xs = X[:, :, S:N].rearrange("p k (b t) -> p k b t", b=NB)
                zs = Z[:, :, S:N].rearrange("p k (b t) -> p k b t", b=NB)
                if s > 0:
                    dve.wait_ge(hh_ready, 4 * s)
                step(dve.tensor_tensor(zs, xs, samples(3 * s + 1), ALU.mult))
                step(dve.tensor_tensor(zs, zs, samples(3 * s), ALU.add))
                for j in range(4):
                    for k in (2 * j, 2 * j + 1):
                        m = dve.tensor_scalar(Z[:, k, 0:S], X[:, k, 0:S], mod[:, (3 * s + 1) * KT + k, 0:1],
                                              mod[:, 3 * s * KT + k, 0:1], ALU.mult, ALU.add)
                    m.then_inc(h_ready, 1)
                for j in range(4):
                    dve.wait_ge(hh_ready, 4 * s + j + 1)
                    dve.tensor_tensor(Hl[:, 2 * j:2 * j + 2, :], Z[:, 2 * j:2 * j + 2, :],
                                      f32(Hh[:, 2 * j:2 * j + 2, :]), ALU.subtract).then_inc(hl_ready, 1)

            def residual(k, bank, g, last, done):
                one = lambda v: v.rearrange("p o n -> p (o n)")
                if isinstance(k, int):
                    zk, xk = Z[:, k, :], X[:, k, :]
                    gp, gs = mod[:, g * KT + k, 0:1], mod[:, g * KT + k, 1:NC]
                else:
                    zk, xk = one(Z[:, bass.ds(k, 1), :]), one(X[:, bass.ds(k, 1), :])
                    gp = one(mod[:, bass.ds(k + g * KT, 1), 0:1])
                    gs = one(mod[:, bass.ds(k + g * KT, 1), 1:NC])
                step(dve.tensor_scalar(zk[:, 0:S], bank[:, 0:S], gp, None, ALU.mult))
                m = dve.tensor_tensor(zk[:, S:N].rearrange("p (b t) -> p b t", b=NB),
                                      bank[:, S:N].rearrange("p (b t) -> p b t", b=NB),
                                      gs.unsqueeze(2).broadcast_to([P, NB, T]), ALU.mult)
                if last:
                    m.then_inc(out_read, 1)
                    dve.wait_ge(out_read, done)
                else:
                    step(m)
                dve.scalar_tensor_tensor(out=zk, in0=xk, scalar=ALPHA, in1=zk, op0=ALU.mult, op1=ALU.add
                                         ).then_inc(z_ready, 1)

            def norm(s, between=lambda j: None):
                two = lambda v: v.unsqueeze(1).broadcast_to([P, 2, N])
                dve.wait_ge(mean_ready, s + 1)
                for j in range(4):
                    zj = Z[:, 2 * j:2 * j + 2, :]
                    dve.tensor_tensor(zj, zj, two(B[2][:, 0:N]), ALU.subtract).then_inc(d_ready, 1)
                between(0)
                dve.wait_ge(sq_used, 4 * s + 4)
                dve.tensor_scalar(rstd[:, :], B[3][:, 0:N], LN_EPS, None, ALU.add).then_inc(veps_ready, 1)
                dve.wait_ge(std_ready, s + 1)
                step(dve.reciprocal(rstd[:, :], rstd[:, :]))
                for j in range(4):
                    zj = Z[:, 2 * j:2 * j + 2, :]
                    step(dve.tensor_tensor(zj, zj, two(rstd[:, :]), ALU.mult))
                    for k in (2 * j, 2 * j + 1):
                        g, b = PRM_AT["ln_g"] + s * KT + k, PRM_AT["ln_b"] + s * KT + k
                        m = dve.tensor_scalar(X[:, k, :], Z[:, k, :], prmT[:, g:g + 1], prmT[:, b:b + 1],
                                              ALU.mult, ALU.add)
                    if s == 2 and j == 3:
                        m.then_inc(x_final, 1)
                    else:
                        step(m)
                between(1)

            def hidden(k, j, read):
                step(dve.tensor_tensor(hf[:, j, :], sg[:, j, :], B[2 * j][:, 0:N], ALU.mult))
                dve.tensor_tensor(hf[:, j, :], hf[:, j, :], B[2 * j + 1][:, 0:N], ALU.mult).then_inc(out_read, 1)
                dve.wait_ge(out_read, read)
                if isinstance(k, int):
                    gh, gl = Gh[:, k, :], Gl[:, k, :]
                else:
                    gh, gl = [v[:, bass.ds(k, 1), :].rearrange("p o n -> p (o n)") for v in (Gh, Gl)]
                step(dve.tensor_copy(gh, hf[:, j, :]))
                dve.tensor_tensor(gl, hf[:, j, :], f32(gh), ALU.subtract).then_inc(g_ready, 1)

            dve.wait_ge(c_sig, 1)
            dve.tensor_tensor(crow[:, :], crow[:, :], csig[:, :], ALU.mult).then_inc(c_silu, 1)
            dve.wait_ge(c_hi, 1)
            dve.tensor_tensor(cpk[:, :, NC:2 * NC], B[0][:, 0:NC * KT].rearrange("p (k c) -> p k c", k=KT),
                              f32(cpk[:, :, 0:NC]), ALU.subtract).then_inc(out_read, 1)
            dve.wait_ge(prm_T, 1)
            dve.tensor_copy(prmT[:, :], B[1][:, 0:NPRM]).then_inc(out_read, 1)
            dve.wait_ge(out_read, 2)
            for k in range(10):
                low(At(k))
            dve.wait_ge(ada_comb, 8)
            add_bias(6, 0, 0, 2 * KT)
            scale_vec(1)
            dve.wait_ge(x_copied, KT)
            modulate(0)
            with dve.Fori(0, 11) as i:
                step.enter(i, 4)
                for j in range(2):
                    low(At(F1 + 2 * j + 2, i, 4))
                    dve.wait_ge(sig_ready, i * 2 + (j + 1))
                    hidden(i * 2 + j, j, i * 2 + (READ["F1"] + j + 1))
                    low(At(F1 + 2 * j + 3, i, 4))
            step.leave(11)
            dve.wait_ge(ada_comb, 30)
            add_bias(7, 0, 2 * KT, 60)
            gate_vec(2, 0.5)
            scale_vec(4)
            gate_vec(5, 1.0)
            with dve.Fori(0, 4) as i:
                step.enter(i, 2)
                for j in range(4):
                    if j % 2:
                        dve.wait_ge(used, At(O1 + j, i, 4)(lambda m: m + 1))
                        residual(i * 2 + j // 2, B[j // 2], 2, True, i * 2 + (READ["O1"] + j // 2 + 1))
                    low(At(O1 + j + 2, i, 4))
            step.leave(4)
            norm(0, lambda j: [low(At(A2 + 2 + 2 * j)), low(At(A2 + 3 + 2 * j))])
            modulate(1)
            for k in range(6, 8):
                low(At(A2 + k))
            dve.wait_ge(s_gla, 32)
            dve.wait_ge(rg_hi, 1)
            dve.tensor_tensor(wrgl[:, :, :], wrg[:, :, :], f32(wrgh[:, :, :]), ALU.subtract).then_inc(rg_lo, 1)
            dve.wait_ge(ada_comb, 36)
            add_bias(6, 16 * NC, 60, 72)
            scale_vec(7)
            gate_vec(8, 0.5)
            with dve.Fori(0, 2) as i:
                for j in range(4):
                    low(At(MI + j + 2, i, 4, 2))
            low(At(MI + 10))
            low(At(MI + 11))
            dve.wait_ge(z_out, 1)
            b_gk = PRM_AT["b_gk"]
            for c in range(GP):
                step(dve.tensor_scalar(tD[:, c, :], B[5 + c][:, 0:N], prmT[:, b_gk + c:b_gk + c + 1], None, ALU.add))
            dve.scalar_tensor_tensor(out=tE[:, :, :], in0=tD[:, :, :], scalar=-1.0, in1=tD[:, :, :], op0=ALU.mult,
                                     op1=ALU.max).then_inc(g_abs, 1)
            for c in range(8):
                dve.wait_ge(rot_out, c + 1)
                step(dve.tensor_tensor(hf[:, 1, :], B[c % 2][:, 0:N], C("sin"), ALU.mult))
                step(dve.tensor_tensor(M[:, c, :], M[:, c, :], C("cos"), ALU.mult))
                dve.tensor_tensor(M[:, c, :], M[:, c, :], hf[:, 1, :], ALU.add).then_inc(roped, 1)
                dve.wait_ge(roped, c + 1)
            dve.wait_ge(g_ln, 1)
            step(dve.tensor_scalar(tD[:, :, :], tD[:, :, :], 0.0, None, ALU.min))
            step(dve.tensor_tensor(tD[:, :, :], tD[:, :, :], tQ[:, :, :], ALU.subtract))
            for c in range(GP):
                step(dve.tensor_tensor_scan(bb[:, c, :], C("reset"), tD[:, c, :], 0.0, ALU.mult, ALU.add))
            dve.wait_ge(new_hi, 1)
            dve.wait_ge(nat_copied, 6)
            dve.tensor_tensor(vnew[:, 1, :], vn[0:NS, 2, :], f32(vnew[:, 0, :]), ALU.subtract).then_inc(new_lo, 1)
            dve.wait_ge(new_hi, 2)
            dve.tensor_tensor(kT2[:, 1, :, :], M[:, CK:CK + HP, S:N], f32(kT2[:, 0, :, :]), ALU.subtract
                              ).then_inc(new_lo, 1)
            for h in range(H + 2):
                if h < H:
                    m_, pr = psm[:, h % 2, :], pp[h % 2]
                    dve.wait_ge(ps_out, h + 1)
                    if h >= 2:
                        dve.wait_ge(pt_T, h - 1)
                    step(dve.tensor_tensor(pr, B[h % 2][:, 0:3 * P], C("causal"), ALU.add))
                    dve.tensor_reduce(m_[:, 0:1], pr[:, 0:P], X_AXIS, ALU.max).then_inc(dve_step, 1)
                    step.k += 1
                    step(dve.tensor_reduce(m_[:, 1:2], pr[:, P:3 * P], X_AXIS, ALU.max))
                    dve.tensor_scalar(m_[:, 2:4], m_[:, 0:2], -HD ** -0.5, None, ALU.mult).then_inc(ps_max, 1)
                if 1 <= h <= H:
                    g = h - 1
                    m_, pr = psm[:, g % 2, :], pp[g % 2]
                    dve.wait_ge(ps_exp, g + 1)
                    step(dve.reciprocal(m_[:, 6:8], m_[:, 4:6]))
                    dve.tensor_scalar(pr[:, 0:P], pr[:, 0:P], m_[:, 6:7], None, ALU.mult).then_inc(dve_step, 1)
                    step.k += 1
                    dve.tensor_scalar(pr[:, P:3 * P], pr[:, P:3 * P], m_[:, 7:8], None, ALU.mult).then_inc(ps_norm, 1)
                if h >= 3 and h % 2:
                    c = (h - 2) // 2
                    dve.wait_ge(po_hi, c + 1)
                    dve.tensor_tensor(Hl[:, c, 0:S], B[(4, 7)[c % 2]][:, 0:S], f32(Hh[:, c, 0:S]), ALU.subtract
                                      ).then_inc(po_lo, 1)
            dve.wait_ge(po_out, H)
            PS = GK ** -0.5

            def level_diff(lv):
                w = 8 if lv == 0 else 16 << (lv - 1)
                r = 3 if lv == 0 else w // 2 - 1
                ns = N if lv == 0 else S
                if lv == 0:
                    v = [x[:, :, :].rearrange("p c (n w) -> p c n w", w=w) for x in (tD, bb)]
                else:
                    v = [x[:, :, 0:S].rearrange("p c (n w) -> p c n w", w=w) for x in (tD, bb)]
                ref = v[1][:, :, :, r:r + 1].broadcast_to([P, 2, ns // w, w])
                m = dve.tensor_tensor(v[0], v[1], ref, ALU.subtract)
                if lv == 0:
                    m.then_inc(g_D, 1)
                    return
                step(m)
                step(dve.tensor_scalar(tE[:, :, 0:S], tD[:, :, 0:S], 0.0, None, ALU.min))
                dve.tensor_scalar(tD[:, :, 0:S], tD[:, :, 0:S], 0.0, None, ALU.max).then_inc(g_D, 1)

            level_diff(0)
            n = 0
            for lv in range(6):
                ns = N if lv == 0 else S
                dve.wait_ge(g_e, lv + 1)
                if lv >= 1:
                    dve.wait_ge(ga_out, 2 * lv + 1)
                dve.scalar_tensor_tensor(out=tQ[:, :, 0:ns], in0=qgT[:, :, 0:ns], scalar=PS, in1=tE[:, :, 0:ns],
                                         op0=ALU.mult, op1=ALU.mult).then_inc(dve_step, 1)
                step.k += 1
                dve.tensor_tensor(tK[:, :, 0:ns], kgT[:, :, 0:ns], tD[:, :, 0:ns], ALU.mult).then_inc(g_qk, 1)
                dve.wait_ge(g_qk, lv + 1)
                dve.wait_ge(dve_step, step.base + step.k)
                if lv < 5:
                    level_diff(lv + 1)
                    for t in ((0, 1, 2) if lv == 0 else (0, 1)):
                        tn = TILES[t][1]
                        dve.wait_ge(ga_out, n + 1)
                        mk = gmask[0:tn, lv, 0:tn].unsqueeze(1).broadcast_to([tn, GP, tn])
                        dst = att[0:tn, t, :, 0:tn]
                        for odd in range(2):
                            src = B[n % 2 + 2 * odd][0:tn, 0:2 * P].rearrange("p (h i) -> p h i", h=GP)[:, :, 0:tn]
                            to = dst if lv == 0 else masked[0:tn]
                            m = dve.tensor_tensor(to.rearrange("p (h two) i -> p two h i", two=2)[:, odd], src, mk,
                                                  ALU.mult)
                            if lv or not odd:
                                step(m)
                        if lv:
                            m = dve.tensor_tensor(dst, dst, masked[0:tn], ALU.add)
                        m.then_inc(ga_read, 1)
                        n += 1
                        dve.wait_ge(ga_read, n)
            dve.wait_ge(g_e, 7)
            dve.scalar_tensor_tensor(out=tQ[:, :, S:N], in0=qgT[:, :, S:N], scalar=PS, in1=eb, op0=ALU.mult,
                                     op1=ALU.mult).then_inc(g_qk, 1)
            step(dve.tensor_tensor(tD[:, :, 0:S], bb[:, :, 0:S], bb[:, :, S - 1:S].broadcast_to([P, 2, S]), ALU.subtract))
            bs = bb[:, :, S:N].rearrange("p c (b t) -> p c b t", b=NB)
            dve.tensor_tensor(tD[:, :, S:N].rearrange("p c (b t) -> p c b t", b=NB), bs,
                              bs[:, :, :, T - 1:T].broadcast_to([P, 2, NB, T]), ALU.subtract).then_inc(g_D, 1)
            dve.wait_ge(gg_exp, 1)
            step(dve.tensor_scalar(gsil, gsil, 1.0, None, ALU.add))
            step(dve.reciprocal(gsil, gsil))
            step(dve.tensor_tensor(gsil, gsil, ggT, ALU.mult))
            dve.wait_ge(g_e, 8)
            dve.wait_ge(ga_out, 12)
            dve.tensor_tensor(tK[:, :, :], kgT, tE[:, :, :], ALU.mult).then_inc(kd_ready, 1)
            ng = PRM_AT["gla_norm_g"]
            for h in range(GH):
                tmp = (sg, hf)[h % 2][:, 1, :]
                dve.wait_ge(go_ms, h + 1)
                dve.tensor_scalar(tmp, B[h % 2][:, 0:N], RMS_EPS, None, ALU.add).then_inc(go_v, 1)
                dve.wait_ge(go_r, h + 1)
                step(dve.scalar_tensor_tensor(out=tmp, in0=B[2 + h][:, 0:N], scalar=prmT[:, ng:ng + 1], in1=tmp,
                                              op0=ALU.mult, op1=ALU.mult))
                step(dve.tensor_tensor(tmp, tmp, gsil[:, h, :], ALU.mult))
                step(dve.tensor_copy(Hh[:, HP + h, :], tmp))
                dve.tensor_tensor(Hl[:, HP + h, :], tmp, f32(Hh[:, HP + h, :]), ALU.subtract).then_inc(go_done, 1)
            dve.wait_ge(kd_copied, 3)
            bm = C("bmask", NS)
            for b in range(NB + 1):
                if b < NB:
                    if b >= 2:
                        dve.wait_ge(ss_out, b - 1)
                    dve.tensor_scalar(kdm[:, b % 2, :], kdn[0:NS, 2, :], bm[:, b:b + 1], None, ALU.mult
                                      ).then_inc(km_ready, 1)
                if b >= 1:
                    c_ = b - 1
                    dve.wait_ge(ss_out, c_ + 1)
                    src = B[3 + c_ % 2][:, :].rearrange("p (c h v) -> p c h v", c=GP, h=2)
                    for h in range(2):
                        rows = slice(GK * h, GK * h + GK)
                        for c in range(GP):
                            m = dve.scalar_tensor_tensor(out=st[rows, c_, c, :], in0=st[rows, c_, c, :],
                                                         scalar=eb[rows, c, T * c_ + T - 1:T * c_ + T],
                                                         in1=src[rows, c, h, :], op0=ALU.mult, op1=ALU.add)
                    m.then_inc(ss_done, 1)

            def queries_low(t):
                for h in range(2):
                    rows = slice(HD * h, HD * h + HD)
                    q_ = Qb[rows, t.n0 % 2, :].rearrange("p (c s) -> p c s", c=HP)
                    if t.i is None:
                        src = M[rows, CQ:CQ + HP, S + T * t.n0:S + T * t.n0 + T]
                    else:
                        src = M[rows, CQ:CQ + HP, bass.ds(t(lambda b: S + T * b), T)]
                    dve.wait_ge(q_hi, t(lambda b: 2 * b + h + 1))
                    dve.tensor_tensor(q_[:, :, QR + T * h:QR + T * h + T], src, f32(q_[:, :, T * h:T * h + T]),
                                      ALU.subtract).then_inc(q_lo, 1)

            def k_low(t, g):
                b0 = t.n0
                slot = (lambda b: KV + g) if b0 == 0 else (lambda b: kv_slot(b, KSLOT[g]))
                n = slot(b0)
                for p in range(4):
                    dve.wait_ge(hi_ready, t(lambda b: parts_before(slot(b)) + p + 1))
                    dve.tensor_tensor(split_view(wl, n, "k")[:, :, p, :],
                                      B[TP[p % 2]][:, :].rearrange("p (c s) -> p c s", c=HP),
                                      f32(split_view(wh, n, "k")[:, :, p, :]), ALU.subtract).then_inc(lo_ready, 1)

            def scores(t, g):
                ks = slice(512 * g, 512 * (g + 1))
                dve.wait_ge(s_low, t(lambda b: 5 * b + g + 2))
                dve.tensor_tensor(Sc[t.n0 % 2][:, ks], B[g][0:QR, :], slo[:, ks], ALU.add).then_inc(s_sum, 1)

            def own(t):
                dve.wait_ge(s_low, t(lambda b: 5 * b + 1))
                if t.n0 >= 1:
                    dve.wait_ge(ptown_T, t(lambda b: b))
                if t.i is None:
                    mk = own_mask[:, t.n0, :]
                else:
                    mk = own_mask[:, bass.ds(t(lambda b: b), 1), :].rearrange("p o s -> p (o s)")
                dst = Sc[t.n0 % 2][:, PAST:KEYS]
                step(dve.tensor_tensor(dst, B[MB][0:QR, 0:NS], slo[:, PAST:KEYS], ALU.add))
                dve.tensor_tensor(dst, dst, mk, ALU.add).then_inc(s_sum, 1)

            def blocks(t):
                return Sc[(t.n0 - 1) % 2][:, 0:PAST].rearrange("p (n k) -> p n k", n=NBLK)

            def choose(t):
                dve.wait_ge(s_sum, t(lambda b: 5 * b))
                step(dve.tensor_reduce(gate, blocks(t), X_AXIS, ALU.add))
                gm = gate.unsqueeze(1).broadcast_to([QR, NBLK, NBLK])
                gn = gate.unsqueeze(2).broadcast_to([QR, NBLK, NBLK])
                step(dve.tensor_tensor(wins, gm, gn, ALU.is_gt))
                step(dve.tensor_tensor(ties, gm, gn, ALU.is_equal))
                step(dve.tensor_tensor(ties, ties, tie_mask, ALU.mult))
                step(dve.tensor_tensor(wins, wins, ties, ALU.add))
                step(dve.tensor_reduce(rank, wins, X_AXIS, ALU.add))
                step(dve.tensor_scalar(rank, rank, TOPK - 0.5, NEG, ALU.is_gt, ALU.mult))

            def maxima(t):
                if t.n0 >= 1:
                    dve.wait_ge(exp_done, t(lambda b: b))
                step(dve.tensor_reduce(bmax[:, 0:NBLK], blocks(t), X_AXIS, ALU.max))
                step(dve.tensor_tensor(bmax[:, 0:NBLK], bmax[:, 0:NBLK], rank, ALU.add))
                step(dve.tensor_reduce(bmax[:, NBLK:NBLK + 1], Sc[(t.n0 - 1) % 2][:, PAST:KEYS], X_AXIS, ALU.max))
                step(dve.tensor_reduce(mneg, bmax, X_AXIS, ALU.max))
                step(dve.tensor_scalar(nbias[:, NBLK:NBLK + 1], mneg, -HD ** -0.5, None, ALU.mult))
                dve.tensor_scalar(nbias[:, 0:NBLK], rank, nbias[:, NBLK:NBLK + 1], None, ALU.add
                                  ).then_inc(bias_ready, 1)

            def totals(t):
                dve.wait_ge(exp_done, t(lambda b: b + 1))
                step(dve.tensor_reduce(ssum, sums, X_AXIS, ALU.add))
                step(dve.reciprocal(rinv[0:QR], ssum))
                step(dve.tensor_copy(rinv[QR:2 * QR], rinv[0:QR]))

            def probs_low(t):
                for r in range(2):
                    dve.wait_ge(pt_hi, t(lambda b: 3 * (b - 1) + r + 1))
                    dve.tensor_tensor(PT[:, 8 * r:8 * r + 8, QR:2 * QR], B[TP[r]][:, :].rearrange("p (g q) -> p g q", g=8),
                                      f32(PT[:, 8 * r:8 * r + 8, 0:QR]), ALU.subtract).then_inc(pt_lo, 1)
                dve.wait_ge(pt_hi, t(lambda b: 3 * b))
                dve.tensor_tensor(PT[0:NS, NPAGE, QR:2 * QR], B[MB][0:NS, 0:QR], f32(PT[0:NS, NPAGE, 0:QR]),
                                  ALU.subtract).then_inc(pt_lo, 1)

            def v_low(t, g):
                slot = (lambda b: kv_slot(b, VSLOT[g])) if t.n0 < NB else (lambda b: kv_slot(NB, g))
                n = slot(t.n0)
                dve.wait_ge(hi_ready, t(lambda b: split_through(slot(b))))
                dve.tensor_tensor(wl[:, n % 2, :], raw[:, n % R, :], f32(wh[:, n % 2, :]), ALU.subtract
                                  ).then_inc(lo_ready, 1)

            def own_heads(t):
                last = (lambda b: kv_slot(b, 7) + 1) if t.n0 < NB else (lambda b: MO)
                dve.wait_ge(used, t(last))
                dve.scalar_tensor_tensor(out=om, in0=B[OB][:, :], scalar=rinv, in1=C("diag"), op0=ALU.mult,
                                         op1=ALU.mult).then_inc(om_ready, 1)

            def out_low(t):
                dve.wait_ge(o_hi, t(lambda b: b))
                src = B[MB][:, 0:T * HP].rearrange("p (c q) -> p c q", c=HP)
                if t.i is None:
                    ts = slice(S + T * (t.n0 - 1), S + T * t.n0)
                else:
                    ts = bass.ds(t(lambda b: S + T * (b - 1)), T)
                dve.tensor_tensor(Hl[:, 0:HP, ts], src, f32(Hh[:, 0:HP, ts]), ALU.subtract).then_inc(o_lo, 1)

            dve.wait_ge(stored, STORED_MIX * 16)
            dve.wait_ge(sp_done, 2)
            dve.sem_inc(om_ready, 1)
            dve.sem_inc(o_lo, 1)
            queries_low(At(0))
            queries_low(At(1))
            own(At(0))
            for g in range(4):
                k_low(At(0), g)
                scores(At(0), g)

            def kv_iteration(t, nxt):
                own(t)
                k_low(t, 0)
                scores(t, 0)
                choose(t)
                k_low(t, 1)
                scores(t, 1)
                maxima(t)
                k_low(t, 2)
                scores(t, 2)
                totals(t)
                probs_low(t)
                v_low(t, 0)
                k_low(t, 3)
                scores(t, 3)
                if nxt is not None:
                    queries_low(nxt)
                for g in range(1, 4):
                    v_low(t, g)
                own_heads(t)
                out_low(t)

            with dve.Fori(0, 3) as i:
                step.enter(i, 2 * 16)
                kv_iteration(At(1, i, 2), At(2, i, 2))
                kv_iteration(At(2, i, 2), At(3, i, 2))
            step.leave(3)
            kv_iteration(At(7), None)
            t = At(NB)
            choose(t)
            maxima(t)
            totals(t)
            probs_low(t)
            for g in range(4):
                v_low(t, g)
            low(At(MO))
            own_heads(t)
            out_low(t)
            low(At(MO + 1))
            for k in range(4):
                dve.wait_ge(used, MO + k + 1)
                residual(2 * k, B[2 * (k % 2)], 5, False, None)
                residual(2 * k + 1, B[2 * (k % 2) + 1], 5, True, READ["MO"] + k + 1)
                low(At(MO + k + 2))
            norm(1)
            modulate(2)
            for k in range(2):
                dve.wait_ge(sig_ready, FC + k + 1)
                hidden(k, k, READ["F2"] + k + 1)
                low(At(F2 + k + 2))
            with dve.Fori(0, 5) as i:
                step.enter(i, 8)
                for j in range(4):
                    dve.wait_ge(sig_ready, i * 4 + (FC + 3 + j))
                    hidden(i * 4 + (2 + j), j % 2, i * 4 + (READ["F2"] + 3 + j))
                    low(At(F2 + 4 + j, i, 4))
            step.leave(5)
            with dve.Fori(0, 3) as i:
                step.enter(i, 2)
                for j in range(4):
                    if j % 2:
                        dve.wait_ge(used, At(O2 + j, i, 4)(lambda m: m + 1))
                        residual(i * 2 + j // 2, B[j // 2], 8, True, i * 2 + (READ["O2"] + j // 2 + 1))
                    low(At(O2 + j + 2, i, 4))
            step.leave(3)
            low(At(O2 + 14))
            dve.wait_ge(used, O2 + 14)
            residual(6, B[0], 8, True, READ["O2"] + 7)
            low(At(O2 + 15))
            dve.wait_ge(used, O2 + 16)
            residual(7, B[1], 8, True, READ["O2"] + 8)
            norm(2)

        @block.gpsimd
        def _(pool):
            step = Steps(pool, pool_step)

            def sum_tiles(s):
                one = lambda v: v.rearrange("p o n -> p (o n)")
                if s:
                    pool.wait_ge(mean_ready, s)
                pool.wait_ge(z_ready, KT * s + 1)
                step(pool.tensor_copy(zsum[:, :], Z[:, 0, :]))
                for k in range(1, KT):
                    pool.wait_ge(z_ready, KT * s + k + 1)
                    m = pool.tensor_tensor(zsum[:, :], zsum[:, :], Z[:, k, :], ALU.add)
                    if k < KT - 1:
                        step(m)
                m.then_inc(zsum_ready, 1)

            sum_tiles(0)
            pool.wait_ge(sq_used, 4)
            step(pool.memset(vgn[NS:P, 2, :], 0.0))
            pool.memset(att[NS:P, 2, :, :], 0.0).then_inc(rows_zero, 1)
            pool.wait_ge(nat_copied, 6)
            pool.dma_start(o["v_prompt"].rearrange("(t p) f -> p t f", p=P), vn[:, 0:2, :]).then_inc(stored, 16)
            pool.dma_start(o["v_sample"], vn[0:NS, 2, :]).then_inc(stored, 16)
            pool.wait_ge(nat_copied, 9)
            pool.dma_start(o["k_prompt"].rearrange("(t p) f -> p t f", p=P), kn[:, 0:2, :]).then_inc(stored, 16)
            pool.dma_start(o["k_sample"], kn[0:NS, 2, :]).then_inc(stored, 16)
            pool.wait_ge(sp_done, 2)
            pool.dma_start(o["gla_prompt"].rearrange("(c h) k v -> (h k) c v", h=2), stp).then_inc(stored, 16)
            pool.wait_ge(ss_done, NB)
            pool.dma_start(o["gla_sample"].rearrange("(r h) k v -> (h k) r v", h=2),
                           st[:, :, :, :].rearrange("p b c v -> p (b c) v")).then_inc(stored, 16)
            pool.wait_ge(go_done, GH)
            pool.memset(Qb[:, :, :].bitcast(F32), 0.0).then_inc(q_zero, 1)
            sum_tiles(1)
            sum_tiles(2)
            pool.wait_ge(y_copied, 4)
            pool.dma_start(o["y_prompt"].rearrange("(t p) d -> p t d", p=P), xn[:, 0:2, :]).then_inc(stored, 16)
            pool.wait_ge(y_copied, 6)
            pool.dma_start(o["y_sample"], xn[0:NS, 2, :]).then_inc(stored, 16)
            pool.wait_ge(stored, 16 * (STORED_MIX + 2))


_OUTS = {
    "y_prompt": ((S, D), (1, S, D)), "y_sample": ((NS, D), (NB, T, D)),
    "k_prompt": ((S, H * HD), (1, 1, S, H, HD)), "v_prompt": ((S, H * HD), (1, 1, S, H, HD)),
    "gla_prompt": ((GH, GK, GV), (1, 1, GH, GK, GV)),
    "k_sample": ((NS, H * HD), (1, NB, T, H, HD)), "v_sample": ((NS, H * HD), (1, NB, T, H, HD)),
    "gla_sample": ((NB * GH, GK, GV), (1, NB, GH, GK, GV)),
}
_SHAPES = {
    "x_prompt": (S, D), "x_sample": (NS, D), "cache_k": (NPHYS, PAGE, H * HD), "cache_v": (NPHYS, PAGE, H * HD),
    "state_gla": (NB * GH, GK, GV), "page_table": (1, NB * NPAGE), "c_prompt": (1, D), "c_sample": (NB, D),
    "w_ada": (D, NM * D), "b_ada": (NM * D,), "ln_g": (3 * D,), "ln_b": (3 * D,), "w_ffn1_in": (D, 2 * FF),
    "w_ffn1_out": (FF, D), "w_mix_in": (D, MIX), "w_gk_up": (RANK, GH * GK), "b_gk": (GH * GK,),
    "gla_norm_g": (GV,), "w_mix_out": (D, D), "w_ffn2_in": (D, 2 * FF), "w_ffn2_out": (FF, D),
}


def kernel(**inputs):
    import concourse.bacc as _bacc
    from concourse.bass_utils import run_bass_kernel_spmd as _run

    nc = _bacc.Bacc("TRN2", target_bir_lowering=False, num_devices=1)
    arrays, a, o = {}, {}, {}
    for name, shape in _SHAPES.items():
        v = np.ascontiguousarray(inputs[name]).reshape(shape)
        arrays[f"in_{name}"] = v
        a[name] = nc.dram_tensor(f"in_{name}", shape, mybir.dt.from_np(v.dtype), kind="ExternalInput").ap()
    arrays["ctab"] = CTAB
    a["ctab"] = nc.dram_tensor("ctab", CTAB.shape, F32, kind="ExternalInput").ap()
    for name, (shape, _) in _OUTS.items():
        o[name] = nc.dram_tensor(f"out_{name}", shape, F32, kind="ExternalOutput").ap()
    layer_kernel(nc, a, o)
    r = _run(nc, [arrays], core_ids=[0])
    return tuple(r.results[0][f"out_{name}"].reshape(full) for name, (_, full) in _OUTS.items())
```
